# Optimizing a Trainium2 kernel written in Bass

```python
import jax, jax.numpy as jnp
from jax import lax
import numpy as np

D_MODEL = 1024
BATCH = 1
SEQ = 512
DEPTH = 1

HEAD_DIM = 128
GDN_HEADS = 4
GDN_QK = GDN_HEADS * HEAD_DIM
GDN_V = GDN_HEADS * HEAD_DIM
GDN_CONV = 4
GDN_CHUNK = 64
NSA_HEADS = 4
NSA_KV_GROUPS = 1
NSA_HPG = NSA_HEADS // NSA_KV_GROUPS
NSA_Q = NSA_HEADS * HEAD_DIM
NSA_KV = NSA_KV_GROUPS * HEAD_DIM
CMP_LEN = 32
CMP_STRIDE = 16
SLC_BLOCK = 64
SLC_TOPK = 16
WINDOW = 512
NSA_Q_BLOCK = 64
FORCE_SCORE = 1.0e4
MEM_LEN = 256
XA_HEADS = 4
XA_HEAD_DIM = D_MODEL // XA_HEADS
D_FF = ((8 * D_MODEL // 3 + 255) // 256) * 256
ROPE_THETA = 10000.0
LN_EPS = 1e-5
RMS_EPS = 1e-6
NEG = -1.0e30
ATTN_SCALE = HEAD_DIM ** -0.5
DN_ALPHA = (2 * DEPTH) ** 0.25
DN_BETA = (8 * DEPTH) ** -0.25
IN_SPLITS = (3 * GDN_QK, GDN_V, GDN_HEADS, GDN_HEADS, NSA_Q, 6 * NSA_KV, 3 * NSA_HEADS, D_MODEL, D_MODEL)
N_IN = sum(IN_SPLITS)

kernel_name = "hybrid_gdn_nsa_deepnorm_block"

def layer_norm(x, g, b):
    xf = x.astype(jnp.float32)
    mu = jnp.mean(xf, -1, keepdims=True)
    var = jnp.mean(jnp.square(xf - mu), -1, keepdims=True)
    return ((xf - mu) * lax.rsqrt(var + LN_EPS) * g + b).astype(x.dtype)

def l2norm(x):
    xf = x.astype(jnp.float32)
    return xf * lax.rsqrt(jnp.sum(xf * xf, -1, keepdims=True) + RMS_EPS)

def rope(x, pos):
    half = x.shape[-1] // 2
    inv = ROPE_THETA ** (-jnp.arange(half, dtype=jnp.float32) / half)
    ang = pos.astype(jnp.float32)[..., None] * inv
    cos = jnp.cos(ang)[:, :, None, :]
    sin = jnp.sin(ang)[:, :, None, :]
    xf = x.astype(jnp.float32)
    x1, x2 = xf[..., :half], xf[..., half:]
    return jnp.concatenate([x1 * cos - x2 * sin, x2 * cos + x1 * sin], -1).astype(x.dtype)

def causal_dwconv(x, w):
    k, c = w.shape
    return lax.conv_general_dilated(x, w[:, None, :].astype(x.dtype), window_strides=(1,),
                                    padding=[(k - 1, 0)], dimension_numbers=('NWC', 'WIO', 'NWC'),
                                    feature_group_count=c)

def gated_delta_rule(q, k, v, g, beta):
    bn, h, s, dk = q.shape
    dv = v.shape[-1]
    c = GDN_CHUNK
    n = s // c
    q, k, v = (t.reshape(bn, h, n, c, t.shape[-1]) for t in (q, k, v))
    g, beta = (t.reshape(bn, h, n, c) for t in (g, beta))
    gc = jnp.cumsum(g, axis=-1)
    incl = jnp.tril(jnp.ones((c, c), bool))
    strict = jnp.tril(jnp.ones((c, c), bool), -1)
    decay = jnp.exp(jnp.where(incl, gc[..., :, None] - gc[..., None, :], -jnp.inf))
    k_beta = k * beta[..., None]
    a_mat = jnp.where(strict, jnp.einsum('bhnid,bhnjd->bhnij', k_beta, k) * decay, 0.0)
    eye = jnp.eye(c, dtype=a_mat.dtype)
    t_inv = lax.linalg.triangular_solve(eye + a_mat, jnp.broadcast_to(eye, a_mat.shape),
                                        left_side=True, lower=True, unit_diagonal=True)
    u = jnp.einsum('bhnij,bhnjd->bhnid', t_inv, v * beta[..., None])
    w = jnp.einsum('bhnij,bhnjd->bhnid', t_inv, k_beta * jnp.exp(gc)[..., None])
    attn = jnp.einsum('bhnid,bhnjd->bhnij', q, k) * decay
    q_dec = q * jnp.exp(gc)[..., None]
    g_last = gc[..., -1]
    k_tail = k * jnp.exp(g_last[..., None] - gc)[..., None]

    def step(state, inp):
        q_c, u_c, w_c, a_c, kt_c, gl_c = inp
        v_new = u_c - jnp.einsum('bhid,bhde->bhie', w_c, state)
        o_c = jnp.einsum('bhid,bhde->bhie', q_c, state) + jnp.einsum('bhij,bhje->bhie', a_c, v_new)
        state = state * jnp.exp(gl_c)[..., None, None] + jnp.einsum('bhid,bhie->bhde', kt_c, v_new)
        return state, o_c

    xs = tuple(jnp.moveaxis(t, 2, 0) for t in (q_dec, u, w, attn, k_tail, g_last))
    state0 = jnp.zeros((bn, h, dk, dv), q.dtype)
    _, o = lax.scan(step, state0, xs)
    return jnp.moveaxis(o, 0, 2).reshape(bn, h, s, dv)

def compress(t, pos_emb, w1, w2):
    bn, s, g, dh = t.shape
    r = CMP_LEN // CMP_STRIDE
    n_cmp = s // CMP_STRIDE - r + 1
    seg = t.reshape(bn, s // CMP_STRIDE, CMP_STRIDE, g, dh)
    blk = jnp.concatenate([seg[:, i:i + n_cmp] for i in range(r)], axis=2)
    blk = blk + pos_emb[:, None, :]
    flat = blk.transpose(0, 1, 3, 2, 4).reshape(bn, n_cmp, g, CMP_LEN * dh)
    return jax.nn.silu(flat @ w1) @ w2

def nsa_attention(q, kv6, gates, positions, cmp_pos_k, cmp_pos_v, cmp_k_w1, cmp_k_w2, cmp_v_w1, cmp_v_w2):
    bn, s, _ = q.shape
    g_, hpg, dh = NSA_KV_GROUPS, NSA_HPG, HEAD_DIM
    q = rope(q.reshape(bn, s, NSA_HEADS, dh), positions)
    q = q.reshape(bn, s, g_, hpg, dh).transpose(0, 2, 3, 1, 4)
    kv6 = kv6.reshape(bn, s, 6, g_, dh)
    k_cmp_raw, v_cmp_raw, k_slc, v_slc, k_win, v_win = (kv6[:, :, i] for i in range(6))
    n_cmp = s // CMP_STRIDE - CMP_LEN // CMP_STRIDE + 1
    n_slc = s // SLC_BLOCK
    top_k = min(SLC_TOPK, n_slc)
    cmp_pos = positions[:, CMP_LEN - 1::CMP_STRIDE][:, :n_cmp]
    k_cmp = rope(compress(k_cmp_raw, cmp_pos_k, cmp_k_w1, cmp_k_w2), cmp_pos).transpose(0, 2, 1, 3)
    v_cmp = compress(v_cmp_raw, cmp_pos_v, cmp_v_w1, cmp_v_w2).transpose(0, 2, 1, 3)
    cmp_start = jnp.arange(n_cmp) * CMP_STRIDE
    cmp_end = cmp_start + CMP_LEN - 1
    slc_start = jnp.arange(n_slc) * SLC_BLOCK
    overlap = ((cmp_start[:, None] < slc_start[None, :] + SLC_BLOCK) &
               (cmp_start[:, None] + CMP_LEN > slc_start[None, :])).astype(jnp.float32)
    k_slc = rope(k_slc, positions).transpose(0, 2, 1, 3).reshape(bn, g_, n_slc, SLC_BLOCK * dh)
    v_slc = v_slc.transpose(0, 2, 1, 3).reshape(bn, g_, n_slc, SLC_BLOCK * dh)
    pad = ((0, 0), (0, 0), (WINDOW, 0), (0, 0))
    k_win = jnp.pad(rope(k_win, positions).transpose(0, 2, 1, 3), pad)
    v_win = jnp.pad(v_win.transpose(0, 2, 1, 3), pad)
    gates = jax.nn.sigmoid(gates.astype(jnp.float32)).reshape(bn, s, g_, hpg, 3).transpose(0, 2, 3, 1, 4)
    sel_shape = (bn, g_, NSA_Q_BLOCK, top_k, SLC_BLOCK, dh)

    def block(qb):
        qs = qb * NSA_Q_BLOCK
        t = qs + jnp.arange(NSA_Q_BLOCK)
        qblk = lax.dynamic_slice_in_dim(q, qs, NSA_Q_BLOCK, axis=3)
        gblk = lax.dynamic_slice_in_dim(gates, qs, NSA_Q_BLOCK, axis=3)
        s_c = jnp.einsum('bghqd,bgnd->bghqn', qblk, k_cmp).astype(jnp.float32) * ATTN_SCALE
        valid_c = cmp_end[None, :] <= t[:, None]
        p_c = jnp.where(valid_c, jax.nn.softmax(jnp.where(valid_c, s_c, NEG), -1), 0.0)
        o_c = jnp.einsum('bghqn,bgnd->bghqd', p_c.astype(v_cmp.dtype), v_cmp)
        imp = jnp.einsum('bghqn,nj->bgqj', p_c, overlap)
        cur = t // SLC_BLOCK
        j = jnp.arange(n_slc)[None, :]
        forced = (j == 0) | (j == cur[:, None]) | (j == cur[:, None] - 1)
        imp = jnp.where(forced, FORCE_SCORE, jnp.where(j <= cur[:, None], imp, -1.0))
        _, idx = lax.top_k(imp, top_k)
        flat_idx = idx.reshape(bn, g_, NSA_Q_BLOCK * top_k, 1)
        k_sel = jnp.take_along_axis(k_slc, flat_idx, axis=2).reshape(sel_shape)
        v_sel = jnp.take_along_axis(v_slc, flat_idx, axis=2).reshape(sel_shape)
        s_s = jnp.einsum('bghqd,bgqkld->bghqkl', qblk, k_sel).astype(jnp.float32) * ATTN_SCALE
        key_pos = idx[..., None] * SLC_BLOCK + jnp.arange(SLC_BLOCK)
        mask_s = (key_pos <= t[:, None, None])[:, :, None]
        s_s = jnp.where(mask_s, s_s, NEG).reshape(bn, g_, hpg, NSA_Q_BLOCK, top_k * SLC_BLOCK)
        p_s = jax.nn.softmax(s_s, -1).reshape(bn, g_, hpg, NSA_Q_BLOCK, top_k, SLC_BLOCK)
        o_s = jnp.einsum('bghqkl,bgqkld->bghqd', p_s.astype(v_sel.dtype), v_sel)
        kw = lax.dynamic_slice_in_dim(k_win, qs, NSA_Q_BLOCK + WINDOW, axis=2)
        vw = lax.dynamic_slice_in_dim(v_win, qs, NSA_Q_BLOCK + WINDOW, axis=2)
        kpos = qs - WINDOW + jnp.arange(NSA_Q_BLOCK + WINDOW)
        rel = t[:, None] - kpos[None, :]
        mask_w = (rel >= 0) & (rel < WINDOW) & (kpos[None, :] >= 0)
        s_w = jnp.einsum('bghqd,bgkd->bghqk', qblk, kw).astype(jnp.float32) * ATTN_SCALE
        p_w = jax.nn.softmax(jnp.where(mask_w, s_w, NEG), -1)
        o_w = jnp.einsum('bghqk,bgkd->bghqd', p_w.astype(vw.dtype), vw)
        o = gblk[..., 0:1] * o_c + gblk[..., 1:2] * o_s + gblk[..., 2:3] * o_w
        return o.astype(q.dtype)

    o = lax.map(block, jnp.arange(s // NSA_Q_BLOCK))
    return o.transpose(1, 0, 4, 2, 3, 5).reshape(bn, s, NSA_Q)

def hybrid_mixer(x, positions, w_in, conv_w, a_log, dt_bias, gdn_norm_w, cmp_pos_k, cmp_pos_v,
                 cmp_k_w1, cmp_k_w2, cmp_v_w1, cmp_v_w2, w_up_gdn, w_up_nsa, w_mix_out):
    bn, s, _ = x.shape
    proj = x @ w_in
    split_pts = np.cumsum(IN_SPLITS)[:-1].tolist()
    qkv, z, a, b, q_n, kv6, g_n, gate_a, gate_b = jnp.split(proj, split_pts, axis=-1)
    qkv = jax.nn.silu(causal_dwconv(qkv, conv_w))
    qg, kg, vg = jnp.split(qkv, [GDN_QK, 2 * GDN_QK], axis=-1)
    heads = lambda t: t.reshape(bn, s, GDN_HEADS, HEAD_DIM).transpose(0, 2, 1, 3)
    qg = l2norm(heads(qg)) * (HEAD_DIM ** -0.5)
    kg = l2norm(heads(kg))
    vg = heads(vg).astype(jnp.float32)
    g = -jnp.exp(a_log.astype(jnp.float32)) * jax.nn.softplus(a.astype(jnp.float32) + dt_bias)
    beta = jax.nn.sigmoid(b.astype(jnp.float32))
    o_a = gated_delta_rule(qg, kg, vg, g.transpose(0, 2, 1), beta.transpose(0, 2, 1)).transpose(0, 2, 1, 3)
    zf = z.reshape(bn, s, GDN_HEADS, HEAD_DIM).astype(jnp.float32)
    o_a = o_a * lax.rsqrt(jnp.mean(o_a * o_a, -1, keepdims=True) + RMS_EPS) * gdn_norm_w * jax.nn.silu(zf)
    y_a = o_a.reshape(bn, s, GDN_V).astype(x.dtype) @ w_up_gdn
    o_b = nsa_attention(q_n, kv6, g_n, positions, cmp_pos_k, cmp_pos_v, cmp_k_w1, cmp_k_w2, cmp_v_w1, cmp_v_w2)
    y_b = o_b @ w_up_nsa
    y = jax.nn.sigmoid(gate_a) * y_a + jax.nn.sigmoid(gate_b) * y_b
    return y @ w_mix_out

def memory_cross_attention(x, mem, wq, wk, wv, wo):
    bn, s, _ = x.shape
    q = (x @ wq).reshape(bn, s, XA_HEADS, XA_HEAD_DIM)
    k = (mem @ wk).reshape(bn, -1, XA_HEADS, XA_HEAD_DIM)
    v = (mem @ wv).reshape(bn, -1, XA_HEADS, XA_HEAD_DIM)
    sc = jnp.einsum('bshd,bmhd->bhsm', q, k).astype(jnp.float32) * (XA_HEAD_DIM ** -0.5)
    p = jax.nn.softmax(sc, -1).astype(v.dtype)
    o = jnp.einsum('bhsm,bmhd->bshd', p, v).reshape(bn, s, D_MODEL)
    return o @ wo

def swiglu(x, w_gate, w_up, w_down):
    return (jax.nn.silu(x @ w_gate) * (x @ w_up)) @ w_down

def setup_inputs(seed: int = 0) -> dict:
    key = jax.random.key(seed)
    ks = iter(jax.random.split(key, 40))
    nrm = lambda shape, scale: jax.random.normal(next(ks), shape, jnp.float32) * scale
    L = DEPTH
    x = jax.random.normal(next(ks), (BATCH, SEQ, D_MODEL), jnp.float32)
    mem = jax.random.normal(next(ks), (BATCH, MEM_LEN, D_MODEL), jnp.float32)
    offs = jax.random.randint(next(ks), (BATCH, 1), 0, 4096, jnp.int32)
    positions = offs + jnp.arange(SEQ, dtype=jnp.int32)[None, :]
    dt = jnp.exp(jax.random.uniform(next(ks), (L, GDN_HEADS), jnp.float32, np.log(1e-3), np.log(1e-1)))
    return {
        "x": x,
        "mem": mem,
        "positions": positions,
        "w_in": nrm((L, D_MODEL, N_IN), D_MODEL ** -0.5),
        "gdn_conv_w": nrm((L, GDN_CONV, 3 * GDN_QK), GDN_CONV ** -0.5),
        "gdn_a_log": jnp.log(jax.random.uniform(next(ks), (L, GDN_HEADS), jnp.float32, 1.0, 16.0)),
        "gdn_dt_bias": dt + jnp.log(-jnp.expm1(-dt)),
        "gdn_norm_w": 1.0 + nrm((L, HEAD_DIM), 0.02),
        "cmp_pos_k": nrm((L, CMP_LEN, HEAD_DIM), 0.02),
        "cmp_pos_v": nrm((L, CMP_LEN, HEAD_DIM), 0.02),
        "cmp_k_w1": nrm((L, CMP_LEN * HEAD_DIM, HEAD_DIM), (CMP_LEN * HEAD_DIM) ** -0.5),
        "cmp_k_w2": nrm((L, HEAD_DIM, HEAD_DIM), HEAD_DIM ** -0.5),
        "cmp_v_w1": nrm((L, CMP_LEN * HEAD_DIM, HEAD_DIM), (CMP_LEN * HEAD_DIM) ** -0.5),
        "cmp_v_w2": nrm((L, HEAD_DIM, HEAD_DIM), HEAD_DIM ** -0.5),
        "w_up_gdn": nrm((L, GDN_V, D_MODEL), GDN_V ** -0.5),
        "w_up_nsa": nrm((L, NSA_Q, D_MODEL), NSA_Q ** -0.5),
        "w_mix_out": nrm((L, D_MODEL, D_MODEL), D_MODEL ** -0.5 * DN_BETA),
        "ln1_g": 1.0 + nrm((L, D_MODEL), 0.02),
        "ln1_b": nrm((L, D_MODEL), 0.02),
        "xa_wq": nrm((L, D_MODEL, D_MODEL), D_MODEL ** -0.5),
        "xa_wk": nrm((L, D_MODEL, D_MODEL), D_MODEL ** -0.5),
        "xa_wv": nrm((L, D_MODEL, D_MODEL), D_MODEL ** -0.5),
        "xa_wo": nrm((L, D_MODEL, D_MODEL), D_MODEL ** -0.5 * DN_BETA),
        "ln2_g": 1.0 + nrm((L, D_MODEL), 0.02),
        "ln2_b": nrm((L, D_MODEL), 0.02),
        "ffn_w_gate": nrm((L, D_MODEL, D_FF), D_MODEL ** -0.5),
        "ffn_w_up": nrm((L, D_MODEL, D_FF), D_MODEL ** -0.5),
        "ffn_w_down": nrm((L, D_FF, D_MODEL), D_FF ** -0.5 * DN_BETA),
        "ln3_g": 1.0 + nrm((L, D_MODEL), 0.02),
        "ln3_b": nrm((L, D_MODEL), 0.02),
    }

def reference(x, mem, positions, w_in, gdn_conv_w, gdn_a_log, gdn_dt_bias, gdn_norm_w, cmp_pos_k, cmp_pos_v,
              cmp_k_w1, cmp_k_w2, cmp_v_w1, cmp_v_w2, w_up_gdn, w_up_nsa, w_mix_out, ln1_g, ln1_b,
              xa_wq, xa_wk, xa_wv, xa_wo, ln2_g, ln2_b, ffn_w_gate, ffn_w_up, ffn_w_down, ln3_g, ln3_b):
    for l in range(DEPTH):
        y = hybrid_mixer(x, positions, w_in[l], gdn_conv_w[l], gdn_a_log[l], gdn_dt_bias[l], gdn_norm_w[l],
                         cmp_pos_k[l], cmp_pos_v[l], cmp_k_w1[l], cmp_k_w2[l], cmp_v_w1[l], cmp_v_w2[l],
                         w_up_gdn[l], w_up_nsa[l], w_mix_out[l])
        x = layer_norm(DN_ALPHA * x + y, ln1_g[l], ln1_b[l])
        y = memory_cross_attention(x, mem, xa_wq[l], xa_wk[l], xa_wv[l], xa_wo[l])
        x = layer_norm(DN_ALPHA * x + y, ln2_g[l], ln2_b[l])
        y = swiglu(x, ffn_w_gate[l], ffn_w_up[l], ffn_w_down[l])
        x = layer_norm(DN_ALPHA * x + y, ln3_g[l], ln3_b[l])
    return x


_drawn_inputs = setup_inputs


def setup_inputs(seed=0):
    import zlib

    import numpy as np

    out = dict(_drawn_inputs(seed))
    spreads = {}
    factors = {'gdn_norm_w': 22.683,
     'cmp_pos_k': 95.199,
     'cmp_pos_v': 43.053,
     'cmp_k_w1': 4.109,
     'cmp_k_w2': 3.8,
     'ln1_g': 2.762,
     'ln1_b': 2.779,
     'ln2_g': 2.797,
     'ln2_b': 2.749,
     'ln3_g': 20.666,
     'ln3_b': 22.062}
    for name, (base, spread) in spreads.items():
        noise = np.random.default_rng([zlib.crc32(name.encode()), seed]).standard_normal(out[name].shape)
        drawn = base * np.exp(spread * noise) if base else spread * noise
        out[name] = __import__('jax').numpy.asarray(drawn.astype(out[name].dtype))
    for name, factor in factors.items():
        out[name] = (out[name] * factor).astype(out[name].dtype)
    return out
```

```python
from contextlib import ExitStack

import concourse.bass as bass
from concourse import mybir

F32 = mybir.dt.float32
F32R = mybir.dt.float32r
I32 = mybir.dt.int32
ALU = mybir.AluOpType
ACT = mybir.ActivationFunctionType
AX_X = mybir.AxisListType.X

P = 128
NEG = -1.0e30
LN_EPS, RMS_EPS = 1e-5, 1e-6
GDN_CONV = 4
CMP_LEN, CMP_STRIDE = 32, 16
C_LEVEL, C_IDENT, C_UPPER, C_ONES, C_CAUSAL, C_CMPADD, C_CMPVALID, C_COLS = 0, 7, 8, 9, 10, 11, 12, 13
TWO_PI = 6.283185307179586
PI_1, PI_2 = 6.28125, 0.0019350051879882812
PI_3 = TWO_PI - PI_1 - PI_2
ROUND = 12582912.0
PI_SAFE = 3.1415925


class Chunk:

    def __init__(self, first, i=0, stride=0):
        self.first, self.i, self.stride = first, i, stride

    def plus(self, k):
        return Chunk(self.first + k, self.i, self.stride)

    @property
    def slot(self):
        return self.first % 2

    def count(self, extra=0):
        return self.first + extra + self.stride * self.i if self.stride else self.first + extra

    def used(self, extra=0):
        return self.count(extra + 1)

    def slot_loads(self):
        n = 16 * (self.first // 2 + 1)
        return n + 16 * (self.stride // 2) * self.i if self.stride else n


class Chain:

    def __init__(self, eng, sem):
        self.eng, self.sem, self.base, self.n = eng, sem, 0, 0

    def do(self, ins):
        self.n += 1
        ins.then_inc(self.sem, 1)

    def wait(self):
        self.eng.wait_ge(self.sem, self.base + self.n)

    def link(self, ins):
        self.do(ins)
        self.wait()

    def loop(self, i, steps):
        self.start, self.steps = self.base + self.n, steps
        self.base, self.n = self.start + i * steps, 0

    def end_loop(self, times):
        assert self.n == self.steps, (self.n, self.steps)
        self.base, self.n = self.start + times * self.steps, 0


def build(nc, x, mem, positions, w_in, gdn_conv_w, gdn_a_log, gdn_dt_bias, gdn_norm_w, cmp_pos_k, cmp_pos_v,
          cmp_k_w1, cmp_k_w2, cmp_v_w1, cmp_v_w2, w_up_gdn, w_up_nsa, w_mix_out, ln1_g, ln1_b,
          xa_wq, xa_wk, xa_wv, xa_wo, ln2_g, ln2_b, ffn_w_gate, ffn_w_up, ffn_w_down, ln3_g, ln3_b, table, out):
    S, D = x.shape[1], x.shape[2]
    ML = mem.shape[1]
    KD = D // P
    R = S // P
    MR = ML // P
    H = gdn_a_log.shape[1]
    HD = gdn_norm_w.shape[1]
    assert HD == P and S == 512 and H == 4 and R == 4
    FF = ffn_w_gate.shape[2]
    KF = FF // P
    N_CMP = S // CMP_STRIDE - CMP_LEN // CMP_STRIDE + 1
    ALPHA = 2.0 ** 0.25
    XH = 4
    XD = D // XH
    COL_A = 3 * H * HD + H * HD
    COL_QN = COL_A + 2 * H
    COL_GN = COL_QN + H * HD + 6 * HD
    COL_GATE = COL_GN + 3 * H
    CH_CONV, CH_Z, CH_NSA, CH_CMP, CH_COMB, CH_MIX = 0, 6, 8, 13, 17, 29
    CH_XK, CH_XV, CH_XQ, CH_XO, CH_FF, CH_DOWN, CH_END = 33, 37, 41, 45, 49, 71, 82
    TR_CONV, TR_Z, TR_NSA, TR_COMB, TR_MIX = 0, 6, 8, 13, 33
    TR_XK, TR_XV, TR_XQ, TR_XO, TR_FF, TR_DOWN = 39, 43, 45, 49, 55, 77

    ctx = ExitStack()
    with ctx:
        def sem(name):
            return ctx.enter_context(nc.semaphore(name))

        KB = 1024
        base = 16512

        def sb(name, shape, dt, at):
            return nc.alloc_sbuf_tensor_at(name, shape, dt, offset=base + at)

        o = [0]

        def fixed(name, shape, dt=F32):
            n = 4
            for s in shape[1:]:
                n *= s
            t = sb(name, shape, dt, o[0])
            o[0] += (n + 31) // 32 * 32
            return t

        cst = fixed("cst", [P, C_COLS * P + 5])
        vecT = fixed("vecT", [P, 113])
        small = fixed("small", [P, 420])
        rope_at = o[0]
        cosT = fixed("cosT", [P, S])
        sinX = fixed("sinX", [P, S])
        wraw = fixed("wraw", [P, 2, 2048])
        whi = fixed("whi", [P, 2, 2048], F32R)
        wlo = fixed("wlo", [P, 2, 2048], F32R)
        xh = fixed("xh", [P, KD, S], F32R)
        xl = fixed("xl", [P, KD, S], F32R)
        RB = (o[0] + 31) // 32 * 32

        def reg(name, shape, at_kb, dt=F32):
            return sb(name, shape, dt, RB + int(at_kb * KB))

        qkvT = reg("qkvT", [P, 3 * H, S], 0)
        zT = reg("zT", [P, H, S], 24)
        nsaT = reg("nsaT", [P, 10, S], 92)
        xnat = reg("xnat", [P, R, D], 96)
        vec = reg("vec", [113, P], 0)
        posi = reg("posi", [P, S], 2, I32)
        rope_t = [reg(f"rope_t{n}", [P, S], 4 + 2 * n) for n in range(4)]
        abg_raw = reg("abg_raw", [P, KD, P], 52)
        abg_h = reg("abg_h", [P, KD, P], 56, F32R)
        abg_l = reg("abg_l", [P, KD, P], 60, F32R)
        abgT = reg("abgT", [20, S], 64)
        pads = reg("pads", [P, 4, S + 16], 32)
        sq_t = reg("sq_t", [P, 2, S], 48)
        rnorm = reg("rnorm", [P, 2 * H, S], 76)
        rope_q = reg("rope_q", [P, 4, S], 32)
        blk = reg("blk", [P, 2, CMP_LEN, 32], 56)
        hcmp_nat = reg("hcmp_nat", [32, 2, P], 75)
        decay = reg("decay", [P, H, S], 32)
        attnT = reg("attnT", [P, H, S], 40)
        ktail = reg("ktail", [P, H, S], 48)
        vnat = reg("vnat", [P, H, S], 56)
        Yinv = reg("Yinv", [P, H, S], 64)
        expg = reg("expg", [P, 2, S], 72)
        state = reg("state", [P, H, HD], 72)
        vnew = reg("vnew", [P, H, HD], 74)
        kdec = reg("kdec", [P, H, S], 76)
        Xinv = reg("Xinv", [P, H, S], 84)
        Zinv = reg("Zinv", [P, H, S], 16)
        wTneg = reg("wTneg", [P, H, S], 8)
        oT = reg("oT", [P, H, S], 32)
        rms_t = reg("rms_t", [P, H, S], 16)
        oah = reg("oah", [P, H, S], 0, F32R)
        oal = reg("oal", [P, H, S], 8, F32R)
        w2k = reg("w2k", [P, HD], 112)
        w2v = reg("w2v", [P, HD], 112.5)
        vcmp = reg("vcmp", [32, HD], 113)
        stats = reg("stats", [P, 4, 32], 113.5)
        hcmp = reg("hcmp", [P, 2, 32], 114)
        kcmpT = reg("kcmpT", [P, 32], 114.25)
        kcmp_t = reg("kcmp_t", [P, 2, 32], 114.375)
        pcmp = reg("pcmp", [P, R, H, 32], 84)
        pcT = reg("pcT", [32, H, S], 76)
        pnat = [reg(f"pnat{n}", [P, 2, S], at) for n, at in enumerate((56, 60, 72))]
        pT = [reg(f"pT{n}", [P, 2, R, S], at) for n, at in enumerate((40, 0))]
        obh = reg("obh", [P, H, S], 84, F32R)
        obl = reg("obl", [P, H, S], 64, F32R)
        gate = reg("gate", [P, 4, S], 72)
        merge = reg("merge", [P, 4, S], 56)
        yh = reg("yh", [P, KD, S], 24, F32R)
        yl = reg("yl", [P, KD, S], 40, F32R)
        memnat = reg("memnat", [P, MR, D], 16)
        mh = reg("mh", [P, KD, ML], 0, F32R)
        ml = reg("ml", [P, KD, ML], 8, F32R)
        kmT = reg("kmT", [P, KD, ML], 56)
        vm = reg("vm", [P, MR, D], 64)
        qT = reg("qT", [P, KD, S], 24)
        pxnat = [reg(f"pxnat{n}", [P, 2, ML], 16 + 2 * n) for n in range(3)]
        pxT = [reg(f"pxT{n}", [P, 2, MR, S], 40 + 8 * n) for n in range(2)]
        xstats = reg("xstats", [P, 4, 32], 22)
        lnp = {k: reg(f"lnp{k}", [P, 2, D], 64 + 8 * k) for k in (1, 2, 3)}
        hh = reg("hh", [P, KF, S], 0, F32R)
        hl = reg("hl", [P, KF, S], 44, F32R)
        silu_t = sb("silu_t", [P, 2, S], F32, rope_at)
        assert RB + int(114.75 * KB) + base <= nc.sbuf_usable_end, RB + 114.75 * KB + base - nc.sbuf_usable_end

        def sm(a, n):
            return small[:, a:a + n]

        dtb, alog, abg = sm(0, 4), sm(4, 4), sm(8, 80)
        s_x, s_ax, s_e, s_l, s_eb, g16, beta = (sm(88 + 16 * n, 16) for n in range(7))
        gcgl, egc, egl, etail = sm(200, 32), sm(232, 16), sm(248, 16), sm(264, 16)
        gsig = sm(280, 48)
        lnst, lnag, lnsd, lnrs = sm(328, 12), sm(340, 8), sm(348, 4), sm(352, 4)
        cm_a, cm_b = sm(356, 16), sm(372, 16)
        abg_v = abg.rearrange("p (c j) -> p c j", j=20)
        ident = cst[:, C_IDENT * P:(C_IDENT + 1) * P]
        upper = cst[:, C_UPPER * P:(C_UPPER + 1) * P]
        ones = cst[:, C_ONES * P:(C_ONES + 1) * P]
        causal = cst[:, C_CAUSAL * P:(C_CAUSAL + 1) * P]
        cmpadd = cst[:, C_CMPADD * P:(C_CMPADD + 1) * P].rearrange("p (t n) -> p t n", n=32)
        cmpvalid = cst[:, C_CMPVALID * P:(C_CMPVALID + 1) * P].rearrange("p (t n) -> p t n", n=32)
        invf = cst[:, C_COLS * P:C_COLS * P + 1]
        sgn = cst[:, C_COLS * P + 1:C_COLS * P + 2]
        eps_q = cst[:, C_COLS * P + 2:C_COLS * P + 3]
        eps_rms = cst[:, C_COLS * P + 3:C_COLS * P + 4]
        eps_ln = cst[:, C_COLS * P + 4:C_COLS * P + 5]

        banks_all = ctx.enter_context(nc.psum_tensor("banks", [P, 8, 512], F32))
        pb = [banks_all[:, n, :] for n in range(8)]

        w_loaded = [sem("w_loaded0"), sem("w_loaded1")]
        w_hi, w_lo, w_used, tile_ready = sem("w_hi"), sem("w_lo"), sem("w_used"), sem("tile_ready")
        loads_issued = sem("loads_issued")
        act_chain, dve_chain = sem("act_chain"), sem("dve_chain")
        x_loaded, cst_loaded, vec_loaded = sem("x_loaded"), sem("cst_loaded"), sem("vec_loaded")
        abg_loaded, pos_loaded, par_loaded = sem("abg_loaded"), sem("pos_loaded"), sem("par_loaded")

        def act_split(act, n):
            if n.first >= CH_END:
                return
            act.wait_ge(w_loaded[n.slot], n.slot_loads())
            if n.first >= 2 or n.stride:
                act.wait_ge(w_used, n.used(-1))
            act.activation(whi[:, n.slot], wraw[:, n.slot], ACT.Copy).then_inc(w_hi, 1)

        def act_skip(act, chunks):
            act.sem_inc(w_hi, chunks)

        def pool_skip(pool, n):
            pool.wait_ge(w_used, n.used(1))
            pool.sem_inc(w_lo, 1)

        def pool_split(pool, n):
            pool.wait_ge(w_hi, n.count(1))
            pool.tensor_tensor(wlo[:, n.slot], wraw[:, n.slot], whi[:, n.slot].bitcast(F32),
                              ALU.subtract).then_inc(w_lo, 1)

        def load_chunk(sp, n, src, k, cols):
            if n.first >= 2 or n.stride:
                sp.wait_ge(w_lo, n.count(-1))
                if n.stride:
                    sp.sem_inc(loads_issued, 1)
            sp.dma_start(wraw[:, n.slot, 0:k * cols].rearrange("p (k c) -> p k c", k=k), src)\
              .then_inc(w_loaded[n.slot], 16)

        def rows(w):
            return w[0].rearrange("(k p) c -> p k c", p=P)

        def passes(ps, wt, xt, first, last):
            nc.tensor.matmul(ps, wt[1], xt[0], start=first, stop=False)
            nc.tensor.matmul(ps, wt[0], xt[1], start=False, stop=False)
            return nc.tensor.matmul(ps, wt[0], xt[0], start=False, stop=last)

        def pe_chunk_T(pe, n, act_h, act_l, kt, tiles, banks, n_tok, wait_bank):
            cols = tiles * P
            wh = whi[:, n.slot, 0:kt * cols].rearrange("p (k c) -> p k c", k=kt)
            wl = wlo[:, n.slot, 0:kt * cols].rearrange("p (k c) -> p k c", k=kt)
            pe.wait_ge(w_lo, n.count(1))
            for m in range(tiles):
                wait_bank(m)
                for k in range(kt):
                    c = slice(m * P, (m + 1) * P)
                    last = passes(pb[banks[m]][:, 0:n_tok], (wh[:, k, c], wl[:, k, c]),
                                  (act_h[:, k, :], act_l[:, k, :]), k == 0, k == kt - 1)
                last.then_inc(w_used if m == tiles - 1 else tile_ready, 1)

        def pe_chunk_nat(pe, n, act_h, act_l, k0, kt, rts, bank0, first, final, cols=512):
            wh = whi[:, n.slot].rearrange("p (k c) -> p k c", k=kt)
            wl = wlo[:, n.slot].rearrange("p (k c) -> p k c", k=kt)
            pe.wait_ge(w_lo, n.count(1))
            for r in range(rts):
                t = slice(r * P, (r + 1) * P)
                for k in range(kt):
                    a = (act_h[:, k0 + k, t], act_l[:, k0 + k, t])
                    for hf in range(wh.shape[2] // 512):
                        c = slice(hf * 512, (hf + 1) * 512)
                        last = passes(pb[bank0 + r + 4 * hf][:, :], a, (wh[:, k, c], wl[:, k, c]),
                                      first and k == 0, final and k == kt - 1)
                        if final and k == kt - 1 and not (r == rts - 1 and hf == wh.shape[2] // 512 - 1):
                            last.then_inc(tile_ready, 1)
            last.then_inc(w_used, 1)

        turn = {k: (sem(f"turned_{k}"), sem(f"turned_hi_{k}"), sem(f"turned_lo_{k}")) for k in ("x", "mem", "x1", "x2")}

        def pe_turn(pe, key, src, nr, bank0=4):
            ps_ready, hi_done, lo_done = turn[key]
            for k in range(KD):
                if k >= 4:
                    pe.wait_ge(lo_done, k - 3)
                for r in range(nr):
                    last = nc.tensor.transpose(pb[bank0 + k % 4][:, r * P:(r + 1) * P],
                                               src[:, r, k * P:(k + 1) * P], ident)
                last.then_inc(ps_ready, 1)

        def act_turn(act, key, dst, nt, tiles=range(KD), bank0=4):
            ps_ready, hi_done, lo_done = turn[key]
            for k in tiles:
                act.wait_ge(ps_ready, k + 1)
                act.activation(dst[:, k, :], pb[bank0 + k % 4][:, 0:nt], ACT.Copy).then_inc(hi_done, 1)

        def dve_turn(dve, key, hi, dst, nt, bank0=4):
            ps_ready, hi_done, lo_done = turn[key]
            for k in range(KD):
                dve.wait_ge(hi_done, k + 1)
                dve.tensor_tensor(dst[:, k, :], pb[bank0 + k % 4][:, 0:nt], hi[:, k, :].bitcast(F32),
                                  ALU.subtract).then_inc(lo_done, 1)

        vec_ps, vec_done = sem("vec_ps"), sem("vec_done")
        abg_hi, abg_lo, abg_ps, abg_copied = sem("abg_hi"), sem("abg_lo"), sem("abg_ps"), sem("abg_copied")
        abg_zero, abg_t, abg_tcopied = sem("abg_zero"), sem("abg_t"), sem("abg_tcopied")
        conv_raw, conv_done, qkv_done = sem("conv_raw"), sem("conv_done"), sem("qkv_done")
        hn_done = sem("hn_done")
        ident_loaded = sem("ident_loaded")
        g_ready, gc_ps, gc_done, scal_act, scal_dve = (sem(k) for k in ("g_ready", "gc_ps", "gc_done", "scal_act", "scal_dve"))
        rope_arg, rope_act, rope_done = sem("rope_arg"), sem("rope_act"), sem("rope_done")
        z_done = sem("z_done")
        rln_done = sem("rln_done")
        sq_done, sq_ps, rn_done, l2_done = sem("sq_done"), sem("sq_ps"), sem("rn_done"), sem("l2_done")
        kv_ps, kn_done, vn_done = sem("kv_ps"), sem("kn_done"), sem("vn_done")
        gcb_ps, kq_ps, kk_ps = sem("gcb_ps"), sem("kq_ps"), sem("kk_ps")
        dmin_done, dexp_done, dmask_done, expg_done = sem("dmin_done"), sem("dexp_done"), sem("dmask_done"), sem("expg_done")
        attn_done, a2_done, qdec_done = sem("attn_done"), sem("a2_done"), sem("qdec_done")
        z_ps, zi_done, x_ps, xi_done, y_ps, yi_done = (sem(k) for k in ("z_ps", "zi_done", "x_ps", "xi_done", "y_ps", "yi_done"))
        wt_ps, wt_done = sem("wt_ps"), sem("wt_done")
        v_ps, v_done, o_ps, o_done, st_ps, st_done = (sem(k) for k in ("v_ps", "v_done", "o_ps", "o_done", "st_ps", "st_done"))
        oln_done = sem("oln_done")
        osq_done, osq_ps, orn_done, oa_done = (sem(k) for k in ("osq_done", "osq_ps", "orn_done", "oa_done"))
        nsa_copied, nsa_roped, w2_loaded, blk_done = sem("nsa_copied"), sem("nsa_roped"), sem("w2_loaded"), sem("blk_done")
        hc_ps, hc_done, kc_ps, kc_done, vc_done = (sem(k) for k in ("hc_ps", "hc_done", "kc_ps", "kc_done", "vc_done"))
        vs_ps, vs_done = sem("vs_ps"), sem("vs_done")
        cs_ps, cs_exp, cs_p, ct_ps, ct_done, cs_sub = (sem(k) for k in ("cs_ps", "cs_exp", "cs_p", "ct_ps", "ct_done", "cs_sub"))
        act_freed, dve_freed, ob_ready = sem("act_freed"), sem("dve_freed"), sem("ob_ready")
        y_done = sem("y_done")
        xn_loaded, mem_loaded = sem("xn_loaded"), sem("mem_loaded")
        lnp_loaded = {k: sem(f"lnp{k}_loaded") for k in (1, 2, 3)}
        ln_sum = {k: sem(f"ln{k}_sum") for k in (1, 2, 3)}
        ln_var = {k: sem(f"ln{k}_var") for k in (1, 2, 3)}
        ln_std = {k: sem(f"ln{k}_std") for k in (1, 2, 3)}
        ln_done = {k: sem(f"ln{k}_done") for k in (1, 2, 3)}
        km_done, vm_done, q_done, ox_ready, ox_hi, ox_lo = (sem(k) for k in ("km_done", "vm_done", "q_done", "ox_ready", "ox_hi", "ox_lo"))
        ff_silu, ff_done, out_stored = sem("ff_silu"), sem("ff_done"), sem("out_stored")

        class Attention:
            def __init__(self, name, groups, parts, width, key_tiles, scale, probs, probs_T, st):
                self.parts = parts
                self.n, self.width, self.key_tiles, self.scale = groups * R, width, key_tiles, scale
                self.probs, self.probs_T, self.st = probs, probs_T, st.rearrange("p k (s b) -> p k s b", b=2)
                self.s_ps, self.nmax, self.exp, self.scaled, self.t_ps, self.t_done, self.used = (
                    sem(f"{name}_{k}") for k in ("s_ps", "nmax", "exp", "scaled", "t_ps", "t_done", "used"))

        nsa = Attention("nsa", H, 1, lambda t: (t + 1) * P, lambda t: t + 1, HD ** -0.5, pnat, pT, stats[:, :, :])
        xat = Attention("xat", XH // 2, 2, lambda t: ML, lambda t: MR, XD ** -0.5, pxnat, pxT, xstats[:, :, :])

        def pe_attention(pe, at, scores, values, between=None, lag=2):
            for s in range(at.n + lag + 4):
                if between:
                    between(s)
                if s < at.n:
                    if s >= 2:
                        pe.wait_ge(at.exp, s - 1)
                    for b in range(2):
                        last = scores(s // R, b, s % R, pb[4 + 2 * (s % 2) + b])
                    last.then_inc(at.s_ps, 1)
                t = s - lag
                if 0 <= t < at.n:
                    pe.wait_ge(at.scaled, t + 1)
                    if t:
                        pe.wait_ge(at.t_done, t)
                    for b in range(2):
                        for k in range(at.key_tiles(t % R)):
                            last = nc.tensor.transpose(pb[2 + b][:, k * P:(k + 1) * P],
                                                       at.probs[t % 3][:, b, k * P:(k + 1) * P], ident)
                    last.then_inc(at.t_ps, 1)
                for part in range(2):
                    t = s - lag - 1 - 2 * part
                    if 0 <= t < at.n and t % R == R - 1:
                        pe.wait_ge(at.t_done, t + 1)
                        values(t // R, part, at.probs_T[(t // R) % 2])

        def act_attention(act, at, finish):
            for s in range(at.n + 6):
                if s < at.n:
                    act.wait_ge(at.nmax, s + 1)
                    if s >= 3:
                        act.wait_ge(at.t_ps, s - 2)
                    w = at.width(s % R)
                    for b in range(2):
                        last = act.activation(at.probs[s % 3][:, b, 0:w], pb[4 + 2 * (s % 2) + b][:, 0:w], ACT.Exp,
                                              bias=at.st[:, 0, s, b:b + 1], scale=at.scale,
                                              accum_out=at.st[:, 1, s, b:b + 1])
                    last.then_inc(at.exp, 1)
                t = s - 2
                if 0 <= t < at.n:
                    act.wait_ge(at.t_ps, t + 1)
                    g, q = t // R, t % R
                    if g >= 2 and q == 0:
                        act.wait_ge(at.used, at.parts * (g - 1))
                    k = at.key_tiles(q)
                    act.activation(at.probs_T[g % 2][:, :, 0:k, q * P:(q + 1) * P],
                                   banks_all[:, 2:4, 0:k * P].rearrange("p b (k q) -> p b k q", k=k),
                                   ACT.Copy).then_inc(at.t_done, 1)
                for part in range(2):
                    t = s - 3 - 2 * part
                    if 0 <= t < at.n and t % R == R - 1:
                        finish(t // R, part)

        def dve_attention(dve, ch, at, factor, finish):
            for s in range(at.n + 7):
                if s < at.n:
                    w = at.width(s % R)
                    bk = 4 + 2 * (s % 2)
                    dve.wait_ge(at.s_ps, s + 1)
                    ch.link(dve.tensor_reduce(at.st[:, 0, s, :], banks_all[:, bk:bk + 2, 0:w], AX_X, ALU.max))
                    dve.tensor_scalar(at.st[:, 0, s, :], at.st[:, 0, s, :], -at.scale, None, ALU.mult).then_inc(at.nmax, 1)
                t = s - 1
                if 0 <= t < at.n:
                    w = at.width(t % R)
                    dve.wait_ge(at.exp, t + 1)
                    ch.link(dve.reciprocal(at.st[:, 2, t, :], at.st[:, 1, t, :]))
                    f = factor(t // R, t % R)
                    if f is not None:
                        ch.link(dve.tensor_tensor(at.st[:, 2, t, :], at.st[:, 2, t, :], f, ALU.mult))
                    for b in range(2):
                        p = at.probs[t % 3][:, b, 0:w]
                        last = dve.tensor_scalar(p, p, at.st[:, 2, t, b:b + 1], None, ALU.mult)
                    last.then_inc(at.scaled, 1)
                for part in range(2):
                    t = s - 4 - 2 * part
                    if 0 <= t < at.n and t % R == R - 1:
                        finish(t // R, part)

        block = ctx.enter_context(nc.Block())
        out_rows = out.rearrange("a (r p) d -> p (a r) d", p=P)
        x_rows = x.rearrange("a (r p) d -> p (a r) d", p=P)

        @block.sync
        def _(sp):
            ic = slice(C_IDENT * P, (C_IDENT + 1) * P)
            sp.dma_start(cst[:, ic], table[:, ic]).then_inc(ident_loaded, 16)
            for r in range(R):
                sp.dma_start(xnat[:, r, :], x_rows[:, r, :]).then_inc(x_loaded, 16)
            win = rows(w_in)

            def at(start, n):
                return bass.ds(start, n)

            def loads(n0, steps, src, k, cols):
                if steps // 2 > 1:
                    with sp.Fori(0, steps // 2) as i:
                        for j in range(2):
                            load_chunk(sp, Chunk(n0 + j, i, 2), src(i, j), k, cols)
                    rest = range(steps // 2 * 2, steps)
                else:
                    rest = range(steps)
                for s in rest:
                    load_chunk(sp, Chunk(n0 + s), src(s // 2, s % 2), k, cols)

            for s in range(2):
                load_chunk(sp, Chunk(s), win[:, :, s * 256:(s + 1) * 256], KD, 256)
            for c in (slice(0, C_IDENT * P), slice((C_IDENT + 1) * P, C_COLS * P + 5)):
                sp.dma_start(cst[:, c], table[:, c]).then_inc(cst_loaded, 16)
            loads(2, 6, lambda i, j: win[:, :, at(512 + i * 512 + j * 256, 256)], KD, 256)
            loads(CH_NSA, 5, lambda i, j: win[:, :, at(COL_QN + i * 512 + j * 256, 256)], KD, 256)
            for s in range(4):
                w1 = (cmp_k_w1, cmp_v_w1)[s // 2][0].rearrange("(l d) c -> d l c", d=P)
                load_chunk(sp, Chunk(CH_CMP + s), w1[:, 16 * (s % 2):16 * (s % 2) + 16, :], 16, P)
            upa, upb = rows(w_up_gdn), rows(w_up_nsa)
            with sp.Fori(0, 2) as i:
                c = Chunk(CH_COMB, i, 6)
                for g, (col, up) in enumerate(((COL_GATE + D, upb), (COL_GATE, upa))):
                    for j in range(2):
                        load_chunk(sp, c.plus(3 * g + j), win[:, :, at(col + i * 512 + j * 256, 256)], KD, 256)
                    load_chunk(sp, c.plus(3 * g + 2), up[:, :, at(i * 512, 512)], H, 512)

            sp.wait_ge(nsa.used, H)
            sp.dma_start(xnat[:, :, :], x_rows).then_inc(xn_loaded, 16)
            sp.wait_ge(oa_done, H)
            sp.dma_start(memnat[:, :, :], mem.rearrange("a (r p) d -> p (a r) d", p=P)).then_inc(mem_loaded, 16)

            def nat(w):
                w = rows(w)
                return lambda i, j: w[:, 4 * j:4 * j + 4, at(i * 512, 512)]

            def chan(w):
                w = rows(w)
                return lambda i, j: w[:, :, at(i * 512 + j * 256, 256)]

            loads(CH_MIX, 4, nat(w_mix_out), 4, 512)
            loads(CH_XK, 4, chan(xa_wk), KD, 256)
            loads(CH_XV, 4, nat(xa_wv), 4, 512)
            loads(CH_XQ, 4, chan(xa_wq), KD, 256)
            loads(CH_XO, 4, nat(xa_wo), 4, 512)
            wg, wu = rows(ffn_w_gate), rows(ffn_w_up)
            loads(CH_FF, 22, lambda i, j: (wg, wu)[j][:, :, at(i * 256, 256)], KD, 256)
            wd = rows(ffn_w_down)
            for s in range(11):
                load_chunk(sp, Chunk(CH_DOWN + s), wd[:, 2 * s:2 * s + 2, :], 2, 1024)
            for r in range(R):
                sp.wait_ge(ln_done[3], r + 1)
                sp.dma_start(out_rows[:, r, :], xnat[:, r, :]).then_inc(out_stored, 16)
            sp.wait_ge(out_stored, 16 * R)

        @block.gpsimd
        def _(pool):
            with pool.Fori(0, CH_CMP // 2) as i:
                for j in range(2):
                    pool_split(pool, Chunk(j, i, 2))
            pool_split(pool, Chunk(CH_CMP - 1))
            for s in range(4):
                pool_skip(pool, Chunk(CH_CMP + s))
            pool_split(pool, Chunk(CH_COMB))
            n0 = CH_COMB + 1
            for h in range(H):
                pool.wait_ge(dexp_done, h + 1)
                pool.affine_select(out=decay[:, h, :], in_=decay[:, h, :], compare_op=ALU.is_ge, fill=0.0,
                                   base=0, pattern=[[0, R], [1, P]], channel_multiplier=-1).then_inc(dmask_done, 1)
            with pool.Fori(0, (CH_END - n0) // 2) as i:
                for j in range(2):
                    pool_split(pool, Chunk(n0 + j, i, 2))

        @block.tensor
        def _(pe):
            pe.sem_inc(w_used, 1)
            pe.wait_ge(ident_loaded, 16)
            pe.wait_ge(x_loaded, 16 * R)
            pe_turn(pe, "x", xnat, R)
            pe.wait_ge(vec_loaded, 64)
            nc.tensor.transpose(pb[0][:, 0:113], vec[:, :], ident[0:113, 0:113]).then_inc(vec_ps, 1)

            pe.wait_ge(turn["x"][2], KD)
            pe.wait_ge(vec_done, 1)
            with pe.Fori(0, 3) as i:
                for j in range(2):
                    pe_chunk_T(pe, Chunk(CH_CONV + j, i, 2), xh, xl, KD, 2, (2 * j, 2 * j + 1), S,
                               lambda m, j=j: pe.wait_ge(conv_raw, 4 * i + 2 * j + m + 1))
            pe.wait_ge(abg_lo, 1)
            for k in range(KD):
                last = passes(pb[4][:, :], (abg_h[:, k, :], abg_l[:, k, :]), (xh[:, k, :], xl[:, k, :]), k == 0, k == KD - 1)
            last.then_inc(abg_t, 1)
            for j in range(2):
                if j:
                    pe.wait_ge(abg_tcopied, 1)
                    for c in range(R):
                        last = nc.tensor.transpose(pb[5][:, c * 20:(c + 1) * 20], abgT[:, c * P:(c + 1) * P],
                                                   ident[0:20, 0:20])
                    last.then_inc(abg_ps, 1)
                pe_chunk_T(pe, Chunk(CH_Z + j), xh, xl, KD, 2, (2 * j, 2 * j + 1), S,
                           lambda m, j=j: pe.wait_ge(conv_raw, 12 + 2 * j + m + 1))
            pe.wait_ge(z_done, H)
            pe.wait_ge(cst_loaded, 32)
            with pe.Fori(0, 2) as i:
                for j in range(2):
                    pe_chunk_T(pe, Chunk(CH_NSA + j, i, 2), xh, xl, KD, 2, (2 * j, 2 * j + 1), S,
                               lambda m, j=j: pe.wait_ge(nsa_copied, 4 * i + 2 * j + m + 1))
                    for m in range(2):
                        pe.wait_ge(sq_done, 4 * i + 2 * j + m + 1)
                        nc.tensor.matmul(pb[6 + m][:, :], ones, sq_t[:, m, :], start=True, stop=True).then_inc(sq_ps, 1)
            pe.wait_ge(g_ready, 1)
            nc.tensor.matmul(pb[5][:, 0:16], upper, g16, start=True, stop=True)
            nc.tensor.matmul(pb[5][:, 16:32], ones, g16, start=True, stop=True).then_inc(gc_ps, 1)
            pe_chunk_T(pe, Chunk(CH_NSA + 4), xh, xl, KD, 2, (0, 1), S,
                       lambda m: pe.wait_ge(nsa_copied, 8 + m + 1))

            def turn_units(bank, tile):
                for c in range(R):
                    last = nc.tensor.transpose(bank[:, c * P:(c + 1) * P], qkvT[:, tile, c * P:(c + 1) * P], ident)
                last.then_inc(kv_ps, 1)

            pe.wait_ge(l2_done, 1)
            pe.wait_ge(nsa_copied, 14)
            for h in range(H):
                turn_units(pb[h], H + h)
            pe.wait_ge(rln_done, 2 * H)
            for s in range(4):
                n = Chunk(CH_CMP + s)
                a, half = s // 2, s % 2
                pe.wait_ge(w_loaded[n.slot], n.slot_loads())
                pe.wait_ge(blk_done, 1 + 2 * (a + 1))
                w = wraw[:, n.slot].rearrange("p (l c) -> p l c", c=P)
                for l in range(16):
                    last = nc.tensor.matmul(pb[7][0:32, a * P:(a + 1) * P], blk[:, a, 16 * half + l, :], w[:, l, :],
                                            start=half == 0 and l == 0, stop=half == 1 and l == 15)
                last.then_inc(w_used, 1)
            pe.wait_ge(abg_copied, 1)
            pe.wait_ge(gc_done, 1)
            for h in range(2):
                turn_units(pb[4 + h], 2 * H + h)
            pe.wait_ge(hn_done, 1)
            for a in range(2):
                last = nc.tensor.transpose(pb[7][:, 256 + 32 * a:256 + 32 * a + N_CMP], hcmp_nat[0:N_CMP, a, :],
                                           ident[0:N_CMP, 0:N_CMP])
            last.then_inc(hc_ps, 1)
            turn_units(pb[6], 2 * H + 2)
            pe.wait_ge(hc_done, 1)
            pe.wait_ge(w2_loaded, 32)
            nc.tensor.matmul(pb[7][:, 320:320 + N_CMP], w2k[:, :], hcmp[:, 0, 0:N_CMP], start=True, stop=True)
            nc.tensor.matmul(pb[7][0:N_CMP, 384:384 + P], hcmp[:, 1, 0:N_CMP], w2v[:, :], start=True, stop=True).then_inc(kc_ps, 1)
            pe.wait_ge(vc_done, 1)
            turn_units(pb[7], 2 * H + 3)
            for h in range(H):
                pe.wait_ge(kn_done, 2 * (h + 1))
                for c in range(R):
                    u = c * H + h
                    last = nc.tensor.matmul(pb[h][:, c * P:(c + 1) * P], g16[:, u:u + 1].to_broadcast([P, P]),
                                            upper, start=True, stop=True)
                last.then_inc(gcb_ps, 1)
                pe.wait_ge(vn_done, h + 1)
                if h == 0:
                    pe.wait_ge(l2_done, 2)
                for c in range(R):
                    t = slice(c * P, (c + 1) * P)
                    last = nc.tensor.matmul(pb[4 + h][:, t], qkvT[:, H + h, t], qkvT[:, h, t], start=True, stop=True)
                last.then_inc(kq_ps, 1)
            for h in range(H):
                pe.wait_ge(dmin_done, h + 1)
                pe.wait_ge(expg_done, h + 1)
                for c in range(R):
                    t = slice(c * P, (c + 1) * P)
                    last = nc.tensor.matmul(pb[h][:, t], qkvT[:, H + h, t], qkvT[:, H + h, t], start=True, stop=True)
                last.then_inc(kk_ps, 1)
            for h in range(H):
                pe.wait_ge(a2_done, h + 1)
                for c in range(R):
                    t = slice(c * P, (c + 1) * P)
                    last = nc.tensor.transpose(pb[h][:, t], decay[:, h, t], ident)
                last.then_inc(z_ps, 1)
            for h in range(H):
                pe.wait_ge(xi_done, h + 1)
                for c in range(R):
                    t = slice(c * P, (c + 1) * P)
                    last = nc.tensor.transpose(pb[h][:, t], Xinv[:, h, t], ident)
                last.then_inc(y_ps, 1)
            with pe.Fori(0, 6) as i:
                for h in range(H):
                    pe.wait_ge(yi_done, 4 * i + h + 1)
                    for c in range(R):
                        t = slice(c * P, (c + 1) * P)
                        last = nc.tensor.matmul(pb[h][:, t], decay[:, h, t], Xinv[:, h, t], start=True, stop=True)
                    last.then_inc(z_ps, 1)
                for h in range(H):
                    pe.wait_ge(zi_done, 4 * i + h + 5)
                    for c in range(R):
                        t = slice(c * P, (c + 1) * P)
                        last = nc.tensor.matmul(pb[4 + h][:, t], Yinv[:, h, t], Zinv[:, h, t], start=True, stop=True)
                    last.then_inc(x_ps, 1)
                for h in range(H):
                    pe.wait_ge(xi_done, 4 * i + h + 5)
                    for c in range(R):
                        t = slice(c * P, (c + 1) * P)
                        last = nc.tensor.transpose(pb[h][:, t], Xinv[:, h, t], ident)
                    last.then_inc(y_ps, 1)
            for h in range(H):
                pe.wait_ge(yi_done, 4 * 6 + h + 1)
                for c in range(R):
                    t = slice(c * P, (c + 1) * P)
                    last = nc.tensor.matmul(pb[4 + h][:, t], kdec[:, h, t], Yinv[:, h, t], start=True, stop=True)
                last.then_inc(wt_ps, 1)
            def head(h):
                return slice(h * P, (h + 1) * P)

            def v_intra(c):
                if c >= 2:
                    pe.wait_ge(v_done, c - 1)
                for h in range(H):
                    t = slice(c * P, (c + 1) * P)
                    last = nc.tensor.matmul(pb[3 * (c % 2)][:, head(h)], Yinv[:, h, t], vnat[:, h, t],
                                            start=h == 0, stop=c == 0 and h == H - 1)
                return last

            def turn_probs(t, bank):
                pe.wait_ge(cs_p, t + 1)
                for h in range(H):
                    last = nc.tensor.transpose(bank[0:32, head(h)], pcmp[:, t, h, :], ident)
                last.then_inc(ct_ps, 1)

            v_intra(0).then_inc(v_ps, 1)
            pe.wait_ge(wt_done, H)
            pe.wait_ge(qdec_done, H)
            for c in range(R):
                t = slice(c * P, (c + 1) * P)
                if c:
                    pe.wait_ge(st_done, H * c)
                    for h in range(H):
                        last = nc.tensor.matmul(pb[3 * (c % 2)][:, head(h)], wTneg[:, h, t], state[:, h, :],
                                                start=False, stop=h == H - 1)
                    last.then_inc(v_ps, 1)
                if c < R - 1:
                    v_intra(c + 1)
                if c < 2:
                    for k in range(R):
                        last = nc.tensor.transpose(pb[6 + c][:, k * P:(k + 1) * P], nsaT[:, 7 + 2 * c, k * P:(k + 1) * P], ident)
                    last.then_inc(vs_ps, 1)
                else:
                    pe.wait_ge(vs_done, c - 1)
                    turn_probs(c - 2, pb[4 + c])
                if c == 0:
                    pe.wait_ge(kc_done, 1)
                    pe.wait_ge(nsa_roped, 3)
                if c >= 2:
                    pe.wait_ge(cs_sub, c - 1)
                for h in range(H):
                    last = nc.tensor.matmul(pb[4 + c % 2][:, h * 32:h * 32 + N_CMP], nsaT[:, h, t],
                                            kcmpT[:, 0:N_CMP], start=True, stop=True)
                last.then_inc(cs_ps, 1)
                if c:
                    pe.wait_ge(o_done, c)
                    for h in range(H):
                        nc.tensor.matmul(pb[1][:, head(h)], state[:, h, :], qkvT[:, h, t], start=h == 0, stop=False)
                pe.wait_ge(v_done, c + 1)
                if c < R - 1:
                    for h in range(H):
                        last = nc.tensor.matmul(pb[2][:, head(h)], ktail[:, h, t], vnew[:, h, :], start=True, stop=True)
                    last.then_inc(st_ps, 1)
                for h in range(H):
                    last = nc.tensor.matmul(pb[1][:, head(h)], vnew[:, h, :], attnT[:, h, t], start=c == 0 and h == 0,
                                            stop=h == H - 1)
                last.then_inc(o_ps, 1)
            pe.wait_ge(cs_sub, R)
            pe.wait_ge(ct_done, 2)

            def between(s):
                if s == 2:
                    for t in (2, 3):
                        turn_probs(t, pb[t])
                    pe.wait_ge(ct_done, R)
                    pe.wait_ge(o_done, R)
                if s == nsa.n + 1:
                    pe.wait_ge(nsa.exp, nsa.n)
                    pe.wait_ge(osq_done, R)
                    for h in range(H):
                        nc.tensor.matmul(pb[4 + h][:, :], ones, rms_t[:, h, :], start=True, stop=True).then_inc(osq_ps, 1)

            def scores(h, b, t, ps):
                w = (t + 1) * P
                nc.tensor.matmul(ps[:, 0:w], nsaT[:, h, t * P:(t + 1) * P], nsaT[:, 6 + 2 * b, 0:w], start=True, stop=False)
                return nc.tensor.matmul(ps[:, w - P:w], ident, causal, start=False, stop=True)

            def values(h, part, pt):
                bank = pb[h % 2]
                if part:
                    return
                if h >= 2:
                    pe.wait_ge(dve_freed, h - 1)
                nc.tensor.matmul(bank[:, :], vcmp[0:N_CMP, :], pcT[0:N_CMP, h, :], start=True, stop=False)
                for b in range(2):
                    for k in range(R):
                        last = nc.tensor.matmul(bank[:, k * P:S], nsaT[:, 7 + 2 * b, k * P:(k + 1) * P], pt[:, b, k, k * P:S],
                                                start=False, stop=b == 1 and k == R - 1)
                last.then_inc(nsa.used, 1)

            pe_attention(pe, nsa, scores, values, between)

            pe.wait_ge(nsa.exp, nsa.n)
            pe.wait_ge(nsa.t_done, nsa.n)
            pe.wait_ge(dve_freed, H)
            pe.wait_ge(oln_done, H)
            with pe.Fori(0, 2) as i:
                for g, (ah, al) in enumerate(((obh, obl), (oah, oal))):
                    c = Chunk(CH_COMB + 3 * g, i, 6)
                    for j in range(2):
                        pe_chunk_T(pe, c.plus(j), xh, xl, KD, 2, (2 * j, 2 * j + 1), S,
                                   lambda m, j=j, g=g: pe.wait_ge(act_freed, 8 * i + 4 * g + 2 * j + m + 1))
                    if g:
                        pe.wait_ge(oa_done, H)
                    pe_chunk_T(pe, c.plus(2), ah, al, H, 4, (4, 5, 6, 7), S,
                               lambda m, g=g: pe.wait_ge(dve_freed, 8 * i + 4 * g + m + 1))

            pe.wait_ge(mem_loaded, 16)
            pe.wait_ge(act_freed, 5 * H)
            pe_turn(pe, "mem", memnat, MR, bank0=0)
            pe.wait_ge(y_done, 4 + KD)
            pe.wait_ge(turn["mem"][2], KD)
            for s in range(4):
                pe_chunk_nat(pe, Chunk(CH_MIX + s), yh, yl, 4 * (s % 2), 4, R, 4 * (s // 2), s % 2 == 0, s % 2 == 1)
            pe.wait_ge(ln_sum[1], R)
            with pe.Fori(0, 2) as i:
                for j in range(2):
                    pe_chunk_T(pe, Chunk(CH_XK + j, i, 2), mh, ml, KD, 2, (2 * j, 2 * j + 1), ML,
                               lambda m, j=j: pe.wait_ge(km_done, 4 * i + 2 * j + m + 1))
            pe.wait_ge(km_done, 12)
            for s in range(4):
                pe_chunk_nat(pe, Chunk(CH_XV + s), mh, ml, 4 * (s % 2), 4, MR, 2 * (s // 2), s % 2 == 0, s % 2 == 1)
            pe.wait_ge(ln_done[1], R)
            pe_turn(pe, "x1", xnat, R)
            pe.wait_ge(vm_done, 4)
            pe.wait_ge(turn["x1"][2], KD)
            with pe.Fori(0, 2) as i:
                for j in range(2):
                    pe_chunk_T(pe, Chunk(CH_XQ + j, i, 2), xh, xl, KD, 2, (2 * j, 2 * j + 1), S,
                               lambda m, j=j: pe.wait_ge(q_done, 4 * i + 2 * j + m + 1))
            pe.wait_ge(q_done, 12)

            def xscores(g, b, t, ps):
                h = 2 * g + b
                for d in range(2):
                    last = nc.tensor.matmul(ps[:, 0:ML], qT[:, 2 * h + d, t * P:(t + 1) * P], kmT[:, 2 * h + d, :],
                                            start=d == 0, stop=d == 1)
                return last

            def xvalues(g, b, pt):
                h = 2 * g + b
                if h:
                    pe.wait_ge(ox_lo, 2 * h)
                for d in range(2):
                    for k in range(MR):
                        c = h * XD + d * P
                        last = nc.tensor.matmul(pb[d][:, :], vm[:, k, c:c + P], pt[:, b, k, :], start=k == 0, stop=k == MR - 1)
                last.then_inc(xat.used, 1)

            pe_attention(pe, xat, xscores, xvalues)
            pe.wait_ge(ox_lo, 2 * XH)
            pe.wait_ge(xat.exp, xat.n)
            for s in range(4):
                pe_chunk_nat(pe, Chunk(CH_XO + s), xh, xl, 4 * (s % 2), 4, R, 4 * (s // 2), s % 2 == 0, s % 2 == 1)
            pe.wait_ge(ln_done[2], R)
            pe_turn(pe, "x2", xnat, R)
            pe.wait_ge(turn["x2"][2], KD)
            with pe.Fori(0, KF // 2) as i:
                pe_chunk_T(pe, Chunk(CH_FF, i, 2), xh, xl, KD, 2, (0, 1), S,
                           lambda m: pe.wait_ge(ff_silu, 2 * i + m + 1))
                pe_chunk_T(pe, Chunk(CH_FF + 1, i, 2), xh, xl, KD, 2, (2, 3), S,
                           lambda m: pe.wait_ge(ff_done, 2 * i + m + 1))
            pe.wait_ge(ff_done, 2 + KF)
            for s in range(11):
                pe_chunk_nat(pe, Chunk(CH_DOWN + s), hh, hl, 2 * s, 2, R, 0, s == 0, s == 10)

        @block.scalar
        def _(act):
            ch = Chain(act, act_chain)
            cw = gdn_conv_w[0].rearrange("i (t c) -> (i t) c", c=P)
            nv = GDN_CONV * 3 * H
            win = rows(w_in)
            act.dma_start(posi[:, :], positions[0].partition_broadcast(P)).then_inc(pos_loaded, 16)
            act.dma_start(vec[0:nv, :], cw).then_inc(vec_loaded, 16)
            act.dma_start(vec[nv:nv + 32, :], cmp_pos_k[0]).then_inc(vec_loaded, 16)
            act.dma_start(vec[nv + 32:nv + 64, :], cmp_pos_v[0]).then_inc(vec_loaded, 16)
            act.dma_start(vec[nv + 64:nv + 65, :], gdn_norm_w).then_inc(vec_loaded, 16)
            act.dma_start(alog, gdn_a_log[0].partition_broadcast(P)).then_inc(par_loaded, 16)
            act.dma_start(dtb, gdn_dt_bias[0].partition_broadcast(P)).then_inc(par_loaded, 16)
            act.dma_start(w2k[:, :], cmp_k_w2[0]).then_inc(w2_loaded, 16)
            act.dma_start(w2v[:, :], cmp_v_w2[0]).then_inc(w2_loaded, 16)
            act.wait_ge(abg_zero, 1)
            act.dma_start(abg_raw[:, :, 0:8], win[:, :, COL_A:COL_A + 8]).then_inc(abg_loaded, 16)
            act.dma_start(abg_raw[:, :, 8:20], win[:, :, COL_GN:COL_GN + 12]).then_inc(abg_loaded, 16)
            act_turn(act, "x", xh, S, range(0, 4))
            act_split(act, Chunk(0))
            act_turn(act, "x", xh, S, range(4, KD))
            act.wait_ge(vec_ps, 1)
            act.activation(vecT[:, :], pb[0][:, 0:113], ACT.Copy).then_inc(vec_done, 1)
            act_split(act, Chunk(1))
            act.wait_ge(rope_arg, 1)
            act.activation(cosT[:, :], rope_t[1][:, :], ACT.Sin).then_inc(rope_act, 1)
            act.activation(sinX[:, :], rope_t[0][:, :], ACT.Sin).then_inc(rope_act, 1)
            act.wait_ge(abg_loaded, 32)
            act.activation(abg_h[:, :, :], abg_raw[:, :, :], ACT.Copy).then_inc(abg_hi, 1)

            def tile_done(n, m, tiles, ready):
                if m == tiles - 1:
                    act.wait_ge(w_used, n.used(1))
                else:
                    act.wait_ge(tile_ready, ready + m + 1)

            act.sem_inc(conv_raw, 4)
            with act.Fori(0, 3) as i:
                for j in range(2):
                    n = Chunk(CH_CONV + j, i, 2)
                    for m in range(2):
                        tile_done(n, m, 2, TR_CONV + 2 * i + j)
                        act.wait_ge(conv_done, 4 * i + 2 * j + m + 1)
                        act.activation(pads[:, 2 * j + m, 16:16 + S], pb[2 * j + m][:, :], ACT.Copy).then_inc(conv_raw, 1)
                    act_split(act, n.plus(2))
            act.wait_ge(abg_t, 1)
            act.activation(abgT[:, :], pb[4][0:20, :], ACT.Copy).then_inc(abg_tcopied, 1)
            for j in range(2):
                n = Chunk(CH_Z + j)
                for m in range(2):
                    tile_done(n, m, 2, TR_Z + j)
                    act.activation(zT[:, 2 * j + m, :], pb[2 * j + m][:, :], ACT.Silu).then_inc(z_done, 1)
                act_split(act, n.plus(2))
                if j == 0:
                    act.wait_ge(conv_done, 4 + 3 * H)
                    for g in range(3):
                        v = qkvT[:, g * H:(g + 1) * H, :]
                        act.activation(v, v, ACT.Silu).then_inc(qkv_done, 1)
            act.wait_ge(scal_dve, 1)
            ch.link(act.activation(s_ax, s_x, ACT.Abs))
            ch.link(act.activation(s_e, s_ax, ACT.Exp, scale=-1.0))
            act.wait_ge(par_loaded, 32)
            ch.link(act.activation(alog, alog, ACT.Exp))
            act.activation(s_eb.rearrange("p (c h) -> p c h", h=H), abg_v[:, :, 4:8], ACT.Exp, scale=-1.0).then_inc(scal_act, 1)
            act.activation(gsig.rearrange("p (c h) -> p c h", h=3 * H), abg_v[:, :, 8:20], ACT.Exp, scale=-1.0).then_inc(scal_act, 1)
            act.activation(s_l, s_e, ACT.Ln, bias=1.0).then_inc(scal_act, 1)
            act.sem_inc(nsa_copied, 4)
            act.wait_ge(qkv_done, 3)
            for i in range(2):
                for j in range(2):
                    n = Chunk(CH_NSA + 2 * i + j)
                    for m in range(2):
                        act.activation(sq_t[:, m, :].unsqueeze(1), qkvT[:, bass.ds(2 * i + m + H * j, 1), :], ACT.Square)\
                           .then_inc(sq_done, 1)
                    for m in range(2):
                        tile_done(n, m, 2, TR_NSA + 2 * i + j)
                        act.activation(nsaT[:, bass.ds(4 * i + 2 * j + m, 1), :], pb[2 * j + m].unsqueeze(1), ACT.Copy)\
                           .then_inc(nsa_copied, 1)
                    if n.first + 2 < CH_CMP:
                        act_split(act, n.plus(2))
                    for m in range(2):
                        act.wait_ge(sq_ps, 4 * i + 2 * j + m + 1)
                        act.activation(rnorm[:, bass.ds(2 * i + m + H * j, 1), :], pb[6 + m].unsqueeze(1), ACT.Ln,
                                       scale=float(HD) if j == 0 else 1.0,
                                       bias=eps_q if j == 0 else eps_rms).then_inc(rln_done, 1)
            act.wait_ge(rln_done, 2 * H)
            for j in (1, 0):
                n = rnorm[:, H * j:H * j + H, :]
                act.activation(n, n, ACT.Exp, scale=-0.5).then_inc(rn_done, 1)
            act.wait_ge(gc_done, 2)
            ch.do(act.activation(egc, gcgl[:, 0:16], ACT.Exp))
            ch.do(act.activation(egl, gcgl[:, 16:32], ACT.Exp))
            act.activation(etail, etail, ACT.Exp).then_inc(scal_act, 1)
            n = Chunk(CH_NSA + 4)
            for m in range(2):
                tile_done(n, m, 2, TR_NSA + 4)
                act.activation(nsaT[:, 8 + m, :], pb[m][:, :], ACT.Copy).then_inc(nsa_copied, 1)
            act_skip(act, 4)
            act.wait_ge(w_used, Chunk(CH_CMP + 3).used(1))
            act.activation(hcmp_nat[0:N_CMP, :, :], pb[7][0:N_CMP, 0:2 * P].rearrange("p (n c) -> p n c", n=2),
                           ACT.Silu).then_inc(hn_done, 1)
            for h in range(H):
                act.wait_ge(kv_ps, H + h + 1)
                act.activation(vnat[:, h, :], pb[4 + h][:, :], ACT.Copy).then_inc(vn_done, 1)
                if h == 0:
                    act.wait_ge(hc_ps, 1)
                    act.activation(hcmp[:, :, 0:N_CMP], pb[7][:, 256:320].rearrange("p (n c) -> p n c", n=2)[:, :, 0:N_CMP],
                                   ACT.Copy).then_inc(hc_done, 1)
                if h >= 2:
                    act_split(act, Chunk(CH_COMB + h - 2))
            for h in range(H):
                act.wait_ge(gcb_ps, h + 1)
                if h >= 2:
                    act.wait_ge(qdec_done, h - 1)
                act.activation(expg[:, h % 2, :], pb[h][:, :], ACT.Exp).then_inc(expg_done, 1)
                act.wait_ge(dmin_done, h + 1)
                act.activation(decay[:, h, :], decay[:, h, :], ACT.Exp).then_inc(dexp_done, 1)
            for h in range(H):
                act.wait_ge(y_ps, h + 1)
                act.activation(Yinv[:, h, :], pb[h][:, :], ACT.Copy).then_inc(yi_done, 1)
            with act.Fori(0, 6) as i:
                for h in range(H):
                    act.wait_ge(y_ps, 4 * i + h + 5)
                    act.activation(Yinv[:, h, :], pb[h][:, :], ACT.Copy).then_inc(yi_done, 1)
            for h in range(H):
                act.wait_ge(wt_ps, h + 1)
                act.activation(wTneg[:, h, :], pb[4 + h][:, :], ACT.Copy, scale=-1.0).then_inc(wt_done, 1)
            def turned_probs(t, bank):
                act.wait_ge(ct_ps, t + 1)
                act.activation(pcT[:, :, t * P:(t + 1) * P], bank[0:32, :].rearrange("p (h q) -> p h q", h=H),
                               ACT.Copy).then_inc(ct_done, 1)

            for c in range(R):
                t = slice(c * P, (c + 1) * P)
                if c < 2:
                    act.wait_ge(vs_ps, c + 1)
                    act.activation(nsaT[:, 7 + 2 * c, :], pb[6 + c][:, :], ACT.Copy).then_inc(vs_done, 1)
                else:
                    turned_probs(c - 2, pb[4 + c])
                act.wait_ge(o_ps, c + 1)
                act.activation(oT[:, :, t], pb[1].rearrange("p (h t) -> p h t", h=H), ACT.Copy).then_inc(o_done, 1)
                act.wait_ge(cs_sub, c + 1)
                act.activation(pcmp[:, c, :, :], pcmp[:, c, :, :], ACT.Exp, scale=HD ** -0.5).then_inc(cs_exp, 1)
                act.wait_ge(o_done, c + 1)
                act.activation(rms_t[:, :, t], oT[:, :, t], ACT.Square).then_inc(osq_done, 1)
            for t in (2, 3):
                turned_probs(t, pb[t])

            def nsa_hi(h, part):
                if part == 0:
                    act.wait_ge(nsa.used, h + 1)
                    act.activation(obh[:, h, :], pb[h % 2][:, :], ACT.Copy).then_inc(act_freed, 1)

            act_attention(act, nsa, nsa_hi)
            for h in range(H):
                act.wait_ge(osq_ps, h + 1)
                act.activation(rms_t[:, h, :], pb[4 + h][:, :], ACT.Ln, scale=1.0 / HD, bias=eps_rms).then_inc(oln_done, 1)
            act.wait_ge(oln_done, H)
            act.activation(rms_t[:, :, :], rms_t[:, :, :], ACT.Exp, scale=-0.5).then_inc(orn_done, 1)

            with act.Fori(0, 2) as i:
                for g in range(2):
                    for j in range(2):
                        n = Chunk(CH_COMB + 3 * g + j, i, 6)
                        for m in range(2):
                            tile_done(n, m, 2, TR_COMB + 10 * i + 5 * g + j)
                            act.wait_ge(dve_freed, 8 * i + 4 * g + 2 * j + m + 1)
                            act.activation(gate[:, 2 * j + m, :], pb[2 * j + m][:, :], ACT.Sigmoid).then_inc(act_freed, 1)
                        act_split(act, n.plus(2))
                    act_split(act, Chunk(CH_COMB + 3 * g + 4, i, 6))
            act_turn(act, "mem", mh, ML, bank0=0)
            act.wait_ge(y_done, 4 + KD)

            def norm_params(k, g, b):
                act.dma_start(lnp[k][:, 0, :], g[0].partition_broadcast(P)).then_inc(lnp_loaded[k], 16)
                act.dma_start(lnp[k][:, 1, :], b[0].partition_broadcast(P)).then_inc(lnp_loaded[k], 16)

            norm_params(1, ln1_g, ln1_b)
            norm_params(2, ln2_g, ln2_b)
            norm_params(3, ln3_g, ln3_b)
            for s in range(4):
                act_split(act, Chunk(CH_MIX + s + 2))

            def std(k, r0, r1):
                act.wait_ge(ln_var[k], r1)
                act.activation(lnsd[:, r0:r1], lnag.rearrange("p (r c) -> p r c", c=2)[:, r0:r1, 1], ACT.Sqrt,
                               bias=eps_ln).then_inc(ln_std[k], 1)

            std(1, 0, R)
            act.sem_inc(km_done, 4)
            with act.Fori(0, 2) as i:
                for j in range(2):
                    n = Chunk(CH_XK + j, i, 2)
                    for m in range(2):
                        tile_done(n, m, 2, TR_XK + 2 * i + j)
                        act.activation(kmT[:, bass.ds(4 * i + 2 * j + m, 1), :], pb[2 * j + m][:, 0:ML].unsqueeze(1),
                                       ACT.Copy).then_inc(km_done, 1)
                    act_split(act, n.plus(2))
            for s in range(4):
                n = Chunk(CH_XV + s)
                if s % 2:
                    for m in range(MR):
                        tile_done(n, m, MR, TR_XV + s // 2)
                        act.activation(vm[:, m, (s // 2) * 512:(s // 2 + 1) * 512], pb[2 * (s // 2) + m][:, :],
                                       ACT.Copy).then_inc(vm_done, 1)
                act_split(act, n.plus(2))
            act_turn(act, "x1", xh, S)
            act.sem_inc(q_done, 4)
            with act.Fori(0, 2) as i:
                for j in range(2):
                    n = Chunk(CH_XQ + j, i, 2)
                    for m in range(2):
                        tile_done(n, m, 2, TR_XQ + 2 * i + j)
                        act.activation(qT[:, bass.ds(4 * i + 2 * j + m, 1), :], pb[2 * j + m].unsqueeze(1),
                                       ACT.Copy).then_inc(q_done, 1)
                    act_split(act, n.plus(2))

            def x_hi(g, b):
                h = 2 * g + b
                act.wait_ge(xat.used, h + 1)
                for d in range(2):
                    act.activation(xh[:, 2 * h + d, :], pb[d][:, :], ACT.Copy).then_inc(ox_hi, 1)

            act_attention(act, xat, x_hi)
            for s in range(4):
                act_split(act, Chunk(CH_XO + s + 2))
            std(2, 0, R)
            act_turn(act, "x2", xh, S)
            act.sem_inc(ff_silu, 2)
            with act.Fori(0, KF // 2) as i:
                for m in range(2):
                    tile_done(Chunk(CH_FF, i, 2), m, 2, TR_FF + 2 * i)
                    act.wait_ge(ff_done, 2 * i + m + 1)
                    act.activation(silu_t[:, m, :], pb[m][:, :], ACT.Silu).then_inc(ff_silu, 1)
                act_split(act, Chunk(CH_FF + 2, i, 2))
                act_split(act, Chunk(CH_FF + 3, i, 2))
            for s in range(9):
                act_split(act, Chunk(CH_DOWN + s + 2))
            for r in range(R):
                std(3, r, r + 1)

        @block.vector
        def _(dve):
            ch = Chain(dve, dve_chain)
            dve.memset(abg_raw[:, :, :], 0.0).then_inc(abg_zero, 1)
            for b in range(4):
                dve.memset(pads[:, b, 0:16], 0.0).then_inc(conv_done, 1)
            dve_turn(dve, "x", xh, xl, S)
            dve.wait_ge(pos_loaded, 16)
            dve.wait_ge(cst_loaded, 32)
            r0, r1, r2, r3 = (t[:, :] for t in rope_t)
            ch.link(dve.tensor_copy(r3, posi[:, :]))
            ch.link(dve.tensor_scalar(r0, r3, invf, None, ALU.mult))
            ch.link(dve.tensor_scalar(r1, r0, 1.0 / TWO_PI, ROUND, ALU.mult, ALU.add))
            ch.link(dve.tensor_scalar(r1, r1, ROUND, None, ALU.subtract))
            for part in (PI_1, PI_2, PI_3):
                ch.link(dve.scalar_tensor_tensor(out=r0, in0=r1, scalar=-part, in1=r0, op0=ALU.mult, op1=ALU.add))
            ch.link(dve.tensor_scalar(r0, r0, PI_SAFE, -PI_SAFE, ALU.min, ALU.max))
            ch.link(dve.tensor_scalar(r2, r0, TWO_PI / 4, None, ALU.add))
            ch.link(dve.tensor_scalar(r3, r2, TWO_PI / 2, -TWO_PI, ALU.is_gt, ALU.mult))
            ch.link(dve.tensor_tensor(r2, r2, r3, ALU.add))
            dve.tensor_scalar(r1, r2, PI_SAFE, -PI_SAFE, ALU.min, ALU.max).then_inc(rope_arg, 1)
            dve.wait_ge(rope_act, 2)
            dve.tensor_scalar(sinX[:, :], sinX[:, :], sgn, None, ALU.mult).then_inc(rope_done, 1)
            dve.wait_ge(abg_hi, 1)
            dve.tensor_tensor(abg_l[:, :, :], abg_raw[:, :, :], abg_h[:, :, :].bitcast(F32), ALU.subtract).then_inc(abg_lo, 1)

            def tile_done(n, m, tiles, ready):
                if m == tiles - 1:
                    dve.wait_ge(w_used, n.used(1))
                else:
                    dve.wait_ge(tile_ready, ready + m + 1)

            dve.wait_ge(vec_done, 1)
            with dve.Fori(0, 3) as i:
                ch.loop(i, 4 * 3)
                for j in range(2):
                    for m in range(2):
                        b = 2 * j + m
                        t = 4 * i + b
                        dst = qkvT[:, bass.ds(t, 1), :]
                        dve.wait_ge(conv_raw, 4 * i + b + 5)
                        ch.link(dve.tensor_scalar(dst, pads[:, b, 13:13 + S].unsqueeze(1), vecT[:, bass.ds(t, 1)], None, ALU.mult))
                        for tap in range(1, GDN_CONV):
                            ins = dve.scalar_tensor_tensor(out=dst, in0=pads[:, b, 13 + tap:13 + tap + S].unsqueeze(1),
                                                           scalar=vecT[:, bass.ds(t + 12 * tap, 1)],
                                                           in1=dst, op0=ALU.mult, op1=ALU.add)
                            if tap < GDN_CONV - 1:
                                ch.link(ins)
                            else:
                                ins.then_inc(conv_done, 1)
            ch.end_loop(3)
            dve.wait_ge(abg_ps, 1)
            dve.tensor_copy(abg, pb[5][:, 0:80]).then_inc(abg_copied, 1)
            dve.wait_ge(abg_copied, 1)
            dve.wait_ge(par_loaded, 32)
            dve.tensor_tensor(s_x.rearrange("p (c h) -> p c h", h=H), abg_v[:, :, 0:4],
                              dtb.unsqueeze(1).to_broadcast([P, R, H]), ALU.add).then_inc(scal_dve, 1)
            dve.wait_ge(scal_act, 3)
            dve.wait_ge(scal_dve, 1)
            ch.link(dve.scalar_tensor_tensor(out=s_x, in0=s_x, scalar=0.0, in1=s_l, op0=ALU.max, op1=ALU.add))
            dve.scalar_tensor_tensor(out=g16.rearrange("p (c h) -> p c h", h=H), in0=s_x.rearrange("p (c h) -> p c h", h=H),
                                     scalar=-1.0, in1=alog.unsqueeze(1).to_broadcast([P, R, H]),
                                     op0=ALU.mult, op1=ALU.mult).then_inc(g_ready, 1)
            ch.link(dve.tensor_scalar(s_eb, s_eb, 1.0, None, ALU.add))
            ch.do(dve.reciprocal(beta, s_eb))
            ch.link(dve.tensor_scalar(gsig, gsig, 1.0, None, ALU.add))
            ch.link(dve.reciprocal(gsig, gsig))

            def rope(x3, cosb, sinb, t, done):
                n2 = P // 2
                ch.do(dve.tensor_tensor(t[0:n2], x3[n2:P], sinb(n2, P), ALU.mult))
                ch.link(dve.tensor_tensor(t[n2:P], x3[0:n2], sinb(0, n2), ALU.mult))
                ch.link(dve.tensor_tensor(x3, x3, cosb, ALU.mult))
                dve.tensor_tensor(x3, x3, t, ALU.add).then_inc(done, 1)

            dve.wait_ge(rope_done, 1)
            dve.wait_ge(conv_done, 4 + 3 * H)
            dve.wait_ge(nsa_copied, 4 + 4)
            rope(nsaT[:, 0:4, :], cosT[:, :].unsqueeze(1).to_broadcast([P, 4, S]),
                 lambda a, b: sinX[a:b, :].unsqueeze(1).to_broadcast([b - a, 4, S]), rope_q[:, :, :], nsa_roped)
            dve.wait_ge(gc_ps, 1)
            dve.tensor_copy(gcgl, pb[5][:, 0:32]).then_inc(gc_done, 1)
            dve.wait_ge(gc_done, 1)
            dve.tensor_tensor(etail, gcgl[:, 16:32], gcgl[:, 0:16], ALU.subtract).then_inc(gc_done, 1)
            nv = GDN_CONV * 3 * H
            dve.memset(blk[:, :, :, N_CMP:32], 0.0).then_inc(blk_done, 1)
            for n in range(2):
                dve.wait_ge(nsa_copied, 4 + 5 + n)
                for a in range(2):
                    seg = nsaT[:, 4 + n, :].rearrange("p (m l) -> p l m", l=CMP_STRIDE)[:, :, a:a + N_CMP]
                    pos = vecT[:, nv + 32 * n + 16 * a:nv + 32 * n + 16 * a + 16].unsqueeze(2).to_broadcast([P, 16, N_CMP])
                    dve.tensor_tensor(blk[:, n, 16 * a:16 * a + 16, 0:N_CMP], seg, pos, ALU.add).then_inc(blk_done, 1)
            dve.wait_ge(nsa_copied, 4 + 7)
            dve.wait_ge(nsa_roped, 1)
            rope(nsaT[:, 6, :], cosT[:, :], lambda a, c: sinX[a:c, :], rope_q[:, 0, :], nsa_roped)
            for n, j in enumerate((1, 0)):
                dve.wait_ge(rn_done, n + 1)
                t = slice(H * j, H * j + H)
                dve.tensor_tensor(qkvT[:, t, :], qkvT[:, t, :], rnorm[:, t, :], ALU.mult).then_inc(l2_done, 1)
            dve.wait_ge(nsa_copied, 4 + 9)
            dve.wait_ge(nsa_roped, 2)
            rope(nsaT[:, 8, :], cosT[:, :], lambda a, c: sinX[a:c, :], rope_q[:, 0, :], nsa_roped)

            def per_unit(v, h):
                return v.rearrange("p (c h) -> p c h", h=H)[:, :, h:h + 1].to_broadcast([P, R, P])

            def units(t):
                return t.rearrange("p (c i) -> p c i", c=R)

            dve.wait_ge(l2_done, 2)
            dve.wait_ge(scal_act, 4)
            for h in range(H):
                dve.wait_ge(kv_ps, h + 1)
                dve.tensor_tensor(units(kdec[:, h, :]), units(pb[h][:, :]), per_unit(egc, h), ALU.mult).then_inc(kn_done, 1)
                dve.tensor_tensor(units(ktail[:, h, :]), units(pb[h][:, :]), per_unit(etail, h), ALU.mult).then_inc(kn_done, 1)
            dve.wait_ge(kc_ps, 1)
            ch.do(dve.tensor_copy(kcmpT[:, 0:N_CMP], pb[7][:, 320:320 + N_CMP]))
            dve.tensor_copy(vcmp[0:N_CMP, :], pb[7][0:N_CMP, 384:384 + P]).then_inc(vc_done, 1)
            ch.wait()
            ends = slice(CMP_LEN - 1, S, CMP_STRIDE)
            rope(kcmpT[:, 0:N_CMP], cosT[:, ends], lambda a, c: sinX[a:c, ends], kcmp_t[:, 0, 0:N_CMP], kc_done)
            dve.wait_ge(nsa_roped, 3)
            for h in range(H):
                dve.wait_ge(expg_done, h + 1)
                for c in range(R):
                    u = c * H + h
                    t = slice(c * P, (c + 1) * P)
                    last = dve.tensor_scalar(decay[:, h, t], pb[h][:, t], gcgl[:, u:u + 1], 0.0, ALU.subtract, ALU.min)
                last.then_inc(dmin_done, 1)
                dve.wait_ge(kq_ps, h + 1)
                dve.tensor_tensor(qkvT[:, h, :], qkvT[:, h, :], expg[:, h % 2, :], ALU.mult).then_inc(qdec_done, 1)
            for h in range(H):
                dve.wait_ge(dmask_done, h + 1)
                ch.link(dve.tensor_tensor(attnT[:, h, :], pb[4 + h][:, :], decay[:, h, :], ALU.mult))
                dve.wait_ge(kk_ps, h + 1)
                for c in range(R):
                    u = c * H + h
                    t = slice(c * P, (c + 1) * P)
                    last = dve.scalar_tensor_tensor(out=decay[:, h, t], in0=pb[h][:, t], scalar=beta[:, u:u + 1],
                                                    in1=decay[:, h, t], op0=ALU.mult, op1=ALU.mult)
                last.then_inc(a2_done, 1)

            def level(l):
                return cst[:, bass.ds(l * P, P)].unsqueeze(1).to_broadcast([P, R, P])

            for h in range(H):
                dve.wait_ge(z_ps, h + 1)
                dve.tensor_tensor(units(Zinv[:, h, :]), units(pb[h][:, :]), level(0), ALU.mult).then_inc(zi_done, 1)
                dve.wait_ge(zi_done, h + 1)
                dve.tensor_tensor(units(Xinv[:, h, :]), ident.unsqueeze(1).to_broadcast([P, R, P]),
                                  units(Zinv[:, h, :]), ALU.subtract).then_inc(xi_done, 1)
            with dve.Fori(0, 6) as i:
                for h in range(H):
                    dve.wait_ge(z_ps, 4 * i + h + 5)
                    dve.tensor_tensor(units(Zinv[:, h, :]), units(pb[h][:, :]), level(i + 1), ALU.mult).then_inc(zi_done, 1)
                for h in range(H):
                    dve.wait_ge(x_ps, 4 * i + h + 1)
                    dve.tensor_tensor(Xinv[:, h, :], Xinv[:, h, :], pb[4 + h][:, :], ALU.subtract).then_inc(xi_done, 1)
            def cmp_scores(t):
                pv = pcmp[:, t, :, 0:N_CMP]
                ma = cm_a[:, 4 * t:4 * t + 4]
                dve.wait_ge(cs_ps, t + 1)
                sc = pb[4 + t % 2][:, 0:P].rearrange("p (h n) -> p h n", h=H)[:, :, 0:N_CMP]
                ch.link(dve.tensor_tensor(pv, sc, cmpadd[:, t:t + 1, 0:N_CMP].to_broadcast([P, H, N_CMP]), ALU.add))
                ch.link(dve.tensor_reduce(ma, pv, AX_X, ALU.max))
                dve.tensor_tensor(pv, pv, ma.unsqueeze(2).to_broadcast([P, H, N_CMP]), ALU.subtract).then_inc(cs_sub, 1)

            def cmp_probs(t):
                pc = pcmp[:, t, :, :]
                pv = pc[:, :, 0:N_CMP]
                ma, mb = cm_a[:, 4 * t:4 * t + 4], cm_b[:, 4 * t:4 * t + 4]
                dve.wait_ge(cs_exp, t + 1)
                ch.link(dve.tensor_reduce(ma, pv, AX_X, ALU.add))
                ch.link(dve.reciprocal(mb, ma))
                g = gsig.rearrange("p (c h b) -> p c h b", h=H, b=3)[:, t, :, 0]
                ch.link(dve.tensor_tensor(mb, mb, g, ALU.mult))
                ch.link(dve.tensor_tensor(pv, pv, mb.unsqueeze(2).to_broadcast([P, H, N_CMP]), ALU.mult))
                dve.tensor_tensor(pc, pc, cmpvalid[:, t:t + 1, :].to_broadcast([P, H, 32]), ALU.mult).then_inc(cs_p, 1)

            for c in range(R):
                dve.wait_ge(v_ps, c + 1)
                if c:
                    dve.wait_ge(o_ps, c)
                dve.tensor_tensor(vnew[:, :, :], pb[3 * (c % 2)][:, :].rearrange("p (h d) -> p h d", h=H),
                                  beta[:, c * H:(c + 1) * H].unsqueeze(2).to_broadcast([P, H, HD]),
                                  ALU.mult).then_inc(v_done, 1)
                if c < R - 1:
                    dve.wait_ge(st_ps, c + 1)
                    for h in range(H):
                        hs = slice(h * P, (h + 1) * P)
                        if c == 0:
                            dve.tensor_copy(state[:, h, :], pb[2][:, hs]).then_inc(st_done, 1)
                        else:
                            if h == 0:
                                dve.wait_ge(st_done, H * c)
                            u = c * H + h
                            dve.scalar_tensor_tensor(out=state[:, h, :], in0=state[:, h, :], scalar=egl[:, u:u + 1],
                                                     in1=pb[2][:, hs], op0=ALU.mult, op1=ALU.add).then_inc(st_done, 1)
                if c == 0:
                    dve.wait_ge(xi_done, 4 * 7)
                    ch.link(dve.memset(pcmp[:, :, :, :], 0.0))
                else:
                    cmp_probs(c - 1)
                cmp_scores(c)
            cmp_probs(R - 1)

            def nsa_lo(h, part):
                if part:
                    return
                dve.wait_ge(act_freed, h + 1)
                dve.tensor_tensor(obl[:, h, :], pb[h % 2][:, :], obh[:, h, :].bitcast(F32), ALU.subtract).then_inc(dve_freed, 1)

            def branch_gate(h, t):
                c = t * 3 * H + 3 * h + 1
                return gsig[:, c:c + 2]

            dve_attention(dve, ch, nsa, branch_gate, nsa_lo)

            dve.wait_ge(orn_done, 1)
            dve.wait_ge(z_done, H)
            for h in range(H):
                rt = rms_t[:, h, :]
                ch.link(dve.scalar_tensor_tensor(out=rt, in0=oT[:, h, :], scalar=vecT[:, 112:113], in1=rt,
                                                 op0=ALU.mult, op1=ALU.mult))
                ch.link(dve.tensor_tensor(oT[:, h, :], rt, zT[:, h, :], ALU.mult))
                ch.link(dve.tensor_copy(oah[:, h, :], oT[:, h, :]))
                dve.tensor_tensor(oal[:, h, :], oT[:, h, :], oah[:, h, :].bitcast(F32), ALU.subtract).then_inc(oa_done, 1)
            dve.sem_inc(y_done, 4)
            with dve.Fori(0, 2) as i:
                ch.loop(i, 4 * 2)
                for g in range(2):
                    n = Chunk(CH_COMB + 3 * g + 2, i, 6)
                    for m in range(4):
                        dve.wait_ge(act_freed, 4 + 8 * i + 4 * g + m + 1)
                        tile_done(n, m, 4, TR_COMB + 10 * i + 5 * g + 2)
                        if g == 0:
                            dve.wait_ge(y_done, 4 * i + m + 1)
                            dve.tensor_tensor(merge[:, m, :], gate[:, m, :], pb[4 + m][:, :], ALU.mult).then_inc(dve_freed, 1)
                        else:
                            ch.link(dve.tensor_tensor(gate[:, m, :], gate[:, m, :], pb[4 + m][:, :], ALU.mult))
                            dve.wait_ge(dve_freed, 4 + 8 * i + m + 1)
                            dve.tensor_tensor(merge[:, m, :], merge[:, m, :], gate[:, m, :], ALU.add).then_inc(dve_freed, 1)
                            dve.wait_ge(dve_freed, 4 + 8 * i + 4 + m + 1)
                            t = bass.ds(4 * i + m, 1)
                            ch.link(dve.tensor_copy(yh[:, t, :], merge[:, m:m + 1, :]))
                            dve.tensor_tensor(yl[:, t, :], merge[:, m:m + 1, :], yh[:, t, :].bitcast(F32),
                                              ALU.subtract).then_inc(y_done, 1)
            ch.end_loop(2)

            def norm(k, tile, by_rows):
                st = lnst.rearrange("p (a b) -> p a b", b=6)

                def total(hf, r):
                    idx, nn = tile(hf, r)
                    if idx is None:
                        dve.wait_ge(w_used, Chunk(nn).used())
                    else:
                        dve.wait_ge(tile_ready, idx)
                    c = slice(hf * 512, (hf + 1) * 512)
                    dve.scalar_tensor_tensor(out=xnat[:, r, c], in0=xnat[:, r, c], scalar=ALPHA,
                                             in1=pb[4 * hf + r][:, :], op0=ALU.mult, op1=ALU.add).then_inc(ln_sum[k], 1)

                def moments(r, n_sums):
                    dve.wait_ge(ln_sum[k], n_sums)
                    for hf in range(2):
                        ch.do(dve.bn_stats(st[:, hf, :], xnat[:, r, hf * 512:(hf + 1) * 512]))
                    ch.wait()
                    dve.bn_aggr(lnag[:, 2 * r:2 * r + 2], lnst).then_inc(ln_var[k], 1)

                def scale(r, n_std):
                    if r == 0:
                        dve.wait_ge(lnp_loaded[k], 32)
                    dve.wait_ge(ln_std[k], n_std)
                    v = xnat[:, r, :]
                    ch.do(dve.reciprocal(lnrs[:, r:r + 1], lnsd[:, r:r + 1]))
                    ch.link(dve.scalar_tensor_tensor(out=v, in0=v, scalar=lnag[:, 2 * r:2 * r + 1], in1=lnp[k][:, 0, :],
                                                     op0=ALU.subtract, op1=ALU.mult))
                    dve.scalar_tensor_tensor(out=v, in0=v, scalar=lnrs[:, r:r + 1], in1=lnp[k][:, 1, :],
                                             op0=ALU.mult, op1=ALU.add).then_inc(ln_done[k], 1)

                if by_rows:
                    for r in range(R):
                        total(0, r)
                        total(1, r)
                        moments(r, 2 * r + 2)
                        if r:
                            dve.wait_ge(ln_var[k], r + 1)
                            scale(r - 1, r)
                        else:
                            dve.wait_ge(ln_var[k], 1)
                    scale(R - 1, R)
                else:
                    for hf in range(2):
                        for r in range(R):
                            total(hf, r)
                            if hf:
                                if r:
                                    dve.wait_ge(ln_var[k], r)
                                moments(r, R + r + 1)
                    for r in range(R):
                        scale(r, 1)

            def proj_order(tr, n0):
                return lambda hf, r: (tr + 3 * hf + r + 1, None) if r < R - 1 else (None, n0 + 2 * hf + 2)

            dve_turn(dve, "mem", mh, ml, ML, bank0=0)
            dve.wait_ge(xn_loaded, 16)
            norm(1, proj_order(TR_MIX, CH_MIX), False)
            dve_turn(dve, "x1", xh, xl, S)
            def x_lo(g, b):
                h = 2 * g + b
                for d in range(2):
                    dve.wait_ge(ox_hi, 2 * h + d + 1)
                    dve.tensor_tensor(xl[:, 2 * h + d, :], pb[d][:, :], xh[:, 2 * h + d, :].bitcast(F32),
                                      ALU.subtract).then_inc(ox_lo, 1)

            dve_attention(dve, ch, xat, lambda g, t: None, x_lo)
            norm(2, proj_order(TR_XO, CH_XO), False)
            dve_turn(dve, "x2", xh, xl, S)
            dve.wait_ge(turn["x2"][2], KD)
            dve.sem_inc(ff_done, 2)
            with dve.Fori(0, KF // 2) as i:
                ch.loop(i, 2 * 2)
                for m in range(2):
                    tile_done(Chunk(CH_FF + 1, i, 2), m, 2, TR_FF + 2 * i + 1)
                    dve.wait_ge(ff_silu, 2 * i + m + 3)
                    ch.link(dve.tensor_tensor(silu_t[:, m, :], silu_t[:, m, :], pb[2 + m][:, :], ALU.mult))
                    t = bass.ds(2 * i + m, 1)
                    ch.link(dve.tensor_copy(hh[:, t, :], silu_t[:, m:m + 1, :]))
                    dve.tensor_tensor(hl[:, t, :], silu_t[:, m:m + 1, :], hh[:, t, :].bitcast(F32),
                                      ALU.subtract).then_inc(ff_done, 1)
            ch.end_loop(KF // 2)
            def down_order(hf, r):
                m = 2 * r + hf
                return (TR_DOWN + m + 1, None) if m < 2 * R - 1 else (None, CH_END)

            norm(3, down_order, True)


_INS = ["x", "mem", "positions", "w_in", "gdn_conv_w", "gdn_a_log", "gdn_dt_bias", "gdn_norm_w", "cmp_pos_k",
        "cmp_pos_v", "cmp_k_w1", "cmp_k_w2", "cmp_v_w1", "cmp_v_w2", "w_up_gdn", "w_up_nsa", "w_mix_out",
        "ln1_g", "ln1_b", "xa_wq", "xa_wk", "xa_wv", "xa_wo", "ln2_g", "ln2_b", "ffn_w_gate", "ffn_w_up",
        "ffn_w_down", "ln3_g", "ln3_b"]


def constant_table():
    import numpy as np
    t = np.zeros((P, C_COLS * P + 5), np.float32)
    i = np.arange(P)[:, None]
    j = np.arange(P)[None, :]
    for l in range(7):
        b = 1 << l
        t[:, l * P:(l + 1) * P] = (i // (2 * b) == j // (2 * b)) & (i // b % 2 == 1) & (j // b % 2 == 0)
    t[:, C_IDENT * P:(C_IDENT + 1) * P] = i == j
    t[:, C_UPPER * P:(C_UPPER + 1) * P] = i <= j
    t[:, C_ONES * P:(C_ONES + 1) * P] = 1.0
    t[:, C_CAUSAL * P:(C_CAUSAL + 1) * P] = np.where(j <= i, 0.0, NEG)
    n = np.arange(32)[None, None, :]
    tok = np.arange(4)[None, :, None] * P + np.arange(P)[:, None, None]
    valid = (CMP_STRIDE * n + CMP_LEN - 1 <= tok) & (n < 31)
    t[:, C_CMPADD * P:(C_CMPADD + 1) * P] = np.where(valid, 0.0, NEG).reshape(P, P)
    t[:, C_CMPVALID * P:(C_CMPVALID + 1) * P] = valid.reshape(P, P)
    half = P // 2
    inv = np.float32(10000.0) ** (-np.arange(half, dtype=np.float32) / np.float32(half))
    t[:, C_COLS * P] = np.concatenate([inv, inv])
    t[:, C_COLS * P + 1] = np.where(np.arange(P) < half, 1.0, -1.0)
    t[:, C_COLS * P + 2:C_COLS * P + 5] = RMS_EPS * P, RMS_EPS, LN_EPS
    return t


def kernel(**inputs):
    import numpy as np
    import concourse.bacc as bacc
    from concourse import mybir as mb
    from concourse.bass_utils import run_bass_kernel_spmd

    nc = bacc.Bacc("TRN2", target_bir_lowering=False, num_devices=1)
    arrays, args = {}, []
    for name in _INS:
        a = np.ascontiguousarray(inputs[name])
        arrays[f"in_{name}"] = a
        args.append(nc.dram_tensor(f"in_{name}", a.shape, mb.dt.from_np(a.dtype), kind="ExternalInput").ap())
    table = constant_table()
    arrays["table"] = table
    args.append(nc.dram_tensor("table", table.shape, mb.dt.float32, kind="ExternalInput").ap())
    shape = tuple(inputs["x"].shape)
    args.append(nc.dram_tensor("out_0", shape, mb.dt.float32, kind="ExternalOutput").ap())
    build(nc, *args)
    r = run_bass_kernel_spmd(nc, [arrays], core_ids=[0])
    return r.results[0]["out_0"]
```
